# Optimizing a Trainium2 kernel written in Bass

```python
import math
import jax, jax.numpy as jnp
from jax import lax
import numpy as np

D_MODEL = 1024
BATCH = 1
SEQ = 256
DEPTH = 2

N_A_LAYERS = DEPTH // 2
N_B_LAYERS = DEPTH - N_A_LAYERS
D_FF = 256 * ((8 * D_MODEL // 3 + 255) // 256)
CONV_WIDTH = 3
HEAD_DIM = 64
N_HEADS = D_MODEL // (2 * HEAD_DIM)
Q_BLOCK = 128
EPS = 1e-6
LAMBDA_STD = 0.1


def rms_norm(x, g):
    xf = x.astype(jnp.float32)
    y = xf * lax.rsqrt(jnp.mean(xf * xf, axis=-1, keepdims=True) + EPS)
    return (y * g.astype(jnp.float32)).astype(x.dtype)

def swiglu(h, w_gate, w_up, w_down):
    return (jax.nn.silu(h @ w_gate) * (h @ w_up)) @ w_down

def short_conv_mixer(h, w_in, w_conv, w_out):
    gate_b, gate_c, u = jnp.split(h @ w_in, 3, axis=-1)
    z = lax.conv_general_dilated(
        gate_c * u, w_conv[:, None, :], window_strides=(1,),
        padding=[(CONV_WIDTH - 1, 0)], dimension_numbers=("NWC", "WIO", "NWC"),
        feature_group_count=D_MODEL)
    return (gate_b * z) @ w_out

def shared_kv(x, g_kv, w_kv):
    b, s, _ = x.shape
    k, v = jnp.split(rms_norm(x, g_kv) @ w_kv, 2, axis=-1)
    k = k.reshape(b, s, N_HEADS, 2, HEAD_DIM)
    v = v.reshape(b, s, N_HEADS, 2 * HEAD_DIM)
    return k, v

def diff_attention(h, k, v, w_q, lq1, lk1, lq2, lk2, g_subln, w_o, lambda_init):
    b, s, _ = h.shape
    q = (h @ w_q).reshape(b, s, N_HEADS, 2, HEAD_DIM) * (HEAD_DIM ** -0.5)
    f32 = jnp.float32
    lam = (jnp.exp(jnp.sum(lq1.astype(f32) * lk1.astype(f32)))
           - jnp.exp(jnp.sum(lq2.astype(f32) * lk2.astype(f32))) + lambda_init)
    n_blocks = s // Q_BLOCK
    q_blocks = jnp.moveaxis(q.reshape(b, n_blocks, Q_BLOCK, N_HEADS, 2, HEAD_DIM), 1, 0)
    key_pos = jnp.arange(s)

    def block(args):
        qb, i = args
        scores = jnp.einsum("bqhcd,bkhcd->bhcqk", qb, k).astype(f32)
        q_pos = i * Q_BLOCK + jnp.arange(Q_BLOCK)
        causal = key_pos[None, :] <= q_pos[:, None]
        p = jax.nn.softmax(jnp.where(causal, scores, -jnp.inf), axis=-1)
        a = p[:, :, 0] - lam * p[:, :, 1]
        return jnp.einsum("bhqk,bkhe->bqhe", a.astype(v.dtype), v)

    o = lax.map(block, (q_blocks, jnp.arange(n_blocks)))
    o = jnp.moveaxis(o, 0, 1).reshape(b, s, N_HEADS, 2 * HEAD_DIM)
    o = rms_norm(o, g_subln) * (1.0 - lambda_init)
    return o.reshape(b, s, D_MODEL) @ w_o

def first_inputs(seed: int = 0) -> dict:
    key = jax.random.key(seed)
    ks = jax.random.split(key, 20)
    f32 = jnp.float32
    nrm = lambda k, shape, fan_in: jax.random.normal(k, shape, f32) * (fan_in ** -0.5)
    return {
        "x": jax.random.normal(ks[0], (BATCH, SEQ, D_MODEL), f32),
        "g_norm": 1.0 + 0.02 * jax.random.normal(ks[1], (DEPTH, 6, D_MODEL), f32),
        "w_ffn_gate": nrm(ks[2], (DEPTH, 2, D_MODEL, D_FF), D_MODEL),
        "w_ffn_up": nrm(ks[3], (DEPTH, 2, D_MODEL, D_FF), D_MODEL),
        "w_ffn_down": nrm(ks[4], (DEPTH, 2, D_FF, D_MODEL), D_FF),
        "w_conv_in": nrm(ks[5], (N_A_LAYERS, D_MODEL, 3 * D_MODEL), D_MODEL),
        "w_conv": nrm(ks[6], (N_A_LAYERS, CONV_WIDTH, D_MODEL), CONV_WIDTH),
        "w_conv_out": nrm(ks[7], (N_A_LAYERS, D_MODEL, D_MODEL), D_MODEL),
        "g_kv": 1.0 + 0.02 * jax.random.normal(ks[8], (D_MODEL,), f32),
        "w_kv": nrm(ks[9], (D_MODEL, 2 * D_MODEL), D_MODEL),
        "w_q": nrm(ks[10], (N_B_LAYERS, D_MODEL, D_MODEL), D_MODEL),
        "lambda_q1": LAMBDA_STD * jax.random.normal(ks[11], (N_B_LAYERS, HEAD_DIM), f32),
        "lambda_k1": LAMBDA_STD * jax.random.normal(ks[12], (N_B_LAYERS, HEAD_DIM), f32),
        "lambda_q2": LAMBDA_STD * jax.random.normal(ks[13], (N_B_LAYERS, HEAD_DIM), f32),
        "lambda_k2": LAMBDA_STD * jax.random.normal(ks[14], (N_B_LAYERS, HEAD_DIM), f32),
        "g_subln": 1.0 + 0.02 * jax.random.normal(ks[15], (N_B_LAYERS, 2 * HEAD_DIM), f32),
        "w_o": nrm(ks[16], (N_B_LAYERS, D_MODEL, D_MODEL), D_MODEL),
    }

def first_block(x, g_norm, w_ffn_gate, w_ffn_up, w_ffn_down, w_conv_in, w_conv, w_conv_out,
              g_kv, w_kv, w_q, lambda_q1, lambda_k1, lambda_q2, lambda_k2, g_subln, w_o):
    k = v = None
    for layer in range(DEPTH):
        g = g_norm[layer]
        f = swiglu(rms_norm(x, g[0]), w_ffn_gate[layer, 0], w_ffn_up[layer, 0], w_ffn_down[layer, 0])
        x = x + 0.5 * rms_norm(f, g[1])
        h = rms_norm(x, g[2])
        if layer < N_A_LAYERS:
            m = short_conv_mixer(h, w_conv_in[layer], w_conv[layer], w_conv_out[layer])
        else:
            j = layer - N_A_LAYERS
            lambda_init = 0.8 - 0.6 * math.exp(-0.3 * layer)
            m = diff_attention(h, k, v, w_q[j], lambda_q1[j], lambda_k1[j], lambda_q2[j],
                               lambda_k2[j], g_subln[j], w_o[j], lambda_init)
        x = x + rms_norm(m, g[3])
        f = swiglu(rms_norm(x, g[4]), w_ffn_gate[layer, 1], w_ffn_up[layer, 1], w_ffn_down[layer, 1])
        x = x + 0.5 * rms_norm(f, g[5])
        if layer == N_A_LAYERS - 1:
            k, v = shared_kv(x, g_kv, w_kv)
    return x


DEPTH_2 = 1

A_HEADS = 4
A_DK = 128
A_DV = 128
A_CHUNK = 64
A_QK_W = A_HEADS * A_DK
A_V_W = A_HEADS * A_DV
B_HEADS = 8
B_KV_GROUPS = 2
B_HPG = B_HEADS // B_KV_GROUPS
B_HEAD_DIM = 64
B_Q_W = B_HEADS * B_HEAD_DIM
B_KV_W = B_KV_GROUPS * B_HEAD_DIM
CMP_LEN = 32
CMP_STRIDE = 16
CMP_HIDDEN = 256
SEL_LEN = 64
SEL_TOPK = 16
WINDOW = 512
FORCE_SCORE = 1e4
NEG = -1e30
ROPE_THETA = 500000.0
ROT_DIM = B_HEAD_DIM // 4
D_FF_2 = 4 * D_MODEL

IN_SIZES = [A_QK_W, A_QK_W, A_V_W, A_V_W,
            B_Q_W, 6 * B_KV_W, 3 * B_HEADS,
            2 * D_MODEL]
N_IN = int(sum(IN_SIZES))
SPLIT_POINTS = [int(v) for v in np.cumsum(IN_SIZES)[:-1]]


def rmsnorm(x, g):
    xf = x.astype(jnp.float32)
    y = xf * lax.rsqrt(jnp.mean(xf * xf, axis=-1, keepdims=True) + EPS) * g.astype(jnp.float32)
    return y.astype(x.dtype)

def masked_softmax(s, mask):
    s = jnp.where(mask, s.astype(jnp.float32), NEG)
    m = jnp.max(s, axis=-1, keepdims=True)
    p = jnp.where(mask, jnp.exp(s - m), 0.0)
    return p / jnp.maximum(jnp.sum(p, axis=-1, keepdims=True), 1e-30)

def partial_rope(t, positions):
    half = ROT_DIM // 2
    inv_freq = ROPE_THETA ** (-jnp.arange(0, ROT_DIM, 2, dtype=jnp.float32) / ROT_DIM)
    ang = positions.astype(jnp.float32)[..., None] * inv_freq
    cos = jnp.cos(ang)[:, :, None, :].astype(t.dtype)
    sin = jnp.sin(ang)[:, :, None, :].astype(t.dtype)
    t1, t2, rest = t[..., :half], t[..., half:ROT_DIM], t[..., ROT_DIM:]
    return jnp.concatenate([t1 * cos - t2 * sin, t2 * cos + t1 * sin, rest], axis=-1)

def hgrn2_mixer(q, f_pre, v, g, lb, norm_g):
    bsz, s, _ = q.shape
    n = s // A_CHUNK
    f32 = jnp.float32
    f = lb + (1.0 - lb) * jax.nn.sigmoid(f_pre.astype(f32))
    k = 1.0 - f

    def heads(t, d):
        return t.astype(f32).reshape(bsz, n, A_CHUNK, A_HEADS, d).transpose(0, 3, 1, 2, 4)

    qh, kh, vh, lfh = heads(q, A_DK), heads(k, A_DK), heads(v, A_DV), heads(jnp.log(f), A_DK)
    b = jnp.cumsum(lfh, axis=3)
    b_last = b[..., -1:, :]
    q_dec = qh * jnp.exp(b)
    k_dec = kh * jnp.exp(-b)
    causal = jnp.tril(jnp.ones((A_CHUNK, A_CHUNK), dtype=bool))
    attn = jnp.where(causal, jnp.einsum('bhnsk,bhntk->bhnst', q_dec, k_dec), 0.0)
    o_intra = jnp.einsum('bhnst,bhntv->bhnsv', attn, vh)
    kv = jnp.einsum('bhntk,bhntv->nbhkv', kh * jnp.exp(b_last - b), vh)
    decay = jnp.exp(b_last[..., 0, :]).transpose(2, 0, 1, 3)

    def step(state, inp):
        dec, kv_n = inp
        return dec[..., None] * state + kv_n, state

    s0 = jnp.zeros((bsz, A_HEADS, A_DK, A_DV), f32)
    _, s_start = lax.scan(step, s0, (decay, kv))
    o_inter = jnp.einsum('bhnsk,nbhkv->bhnsv', q_dec, s_start)
    o = (o_intra + o_inter).transpose(0, 2, 3, 1, 4).reshape(bsz, s, A_HEADS, A_DV)
    o = rmsnorm(o, norm_g) * jax.nn.silu(g.astype(f32).reshape(bsz, s, A_HEADS, A_DV))
    return o.reshape(bsz, s, A_V_W).astype(q.dtype)

def nsa_mixer(q, kc_tok, vc_tok, ks, vs, kw, vw, gate_pre, positions,
              pe_k, pe_v, w1_k, w2_k, w1_v, w2_v):
    bsz, s, _ = q.shape
    G, HPG, HD = B_KV_GROUPS, B_HPG, B_HEAD_DIM

    def kvh(t):
        return t.reshape(bsz, s, G, HD)

    q = partial_rope(q.reshape(bsz, s, B_HEADS, HD), positions)
    kc_tok = partial_rope(kvh(kc_tok), positions)
    vc_tok = kvh(vc_tok)
    ks = partial_rope(kvh(ks), positions)
    kw = partial_rope(kvh(kw), positions)

    n_cmp = (s - CMP_LEN) // CMP_STRIDE + 1
    blk_idx = np.arange(n_cmp)[:, None] * CMP_STRIDE + np.arange(CMP_LEN)[None, :]

    def compress(tok, pe, w1, w2):
        blocks = tok[:, blk_idx] + pe[None, None, :, None, :]
        flat = blocks.transpose(0, 1, 3, 2, 4).reshape(bsz, n_cmp, G, CMP_LEN * HD)
        return (jax.nn.gelu(flat @ w1) @ w2).transpose(0, 2, 1, 3)

    kc = compress(kc_tok, pe_k, w1_k, w2_k)
    vc = compress(vc_tok, pe_v, w1_v, w2_v)
    cmp_end = jnp.asarray(blk_idx[:, -1], jnp.int32)

    n_slc = s // SEL_LEN
    cs = np.arange(n_cmp)[:, None] * CMP_STRIDE
    ss = np.arange(n_slc)[None, :] * SEL_LEN
    overlap = np.clip(np.minimum(cs + CMP_LEN, ss + SEL_LEN) - np.maximum(cs, ss), 0, None) / CMP_LEN
    overlap = jnp.asarray(overlap, jnp.float32)
    n_top = min(SEL_TOPK, n_slc)

    qg = q.reshape(bsz, s, G, HPG, HD).transpose(0, 2, 3, 1, 4) * (HD ** -0.5)
    ks_g = ks.transpose(0, 2, 1, 3)
    vs_g = kvh(vs).transpose(0, 2, 1, 3)
    pad = ((0, 0), (0, 0), (WINDOW, 0), (0, 0))
    kw_pad = jnp.pad(kw.transpose(0, 2, 1, 3), pad)
    vw_pad = jnp.pad(kvh(vw).transpose(0, 2, 1, 3), pad)
    gates = jax.nn.sigmoid(gate_pre.reshape(bsz, s, G, HPG, 3)).transpose(0, 2, 3, 1, 4)
    bi = jnp.arange(bsz)[:, None, None]
    gi = jnp.arange(G)[None, :, None]
    sel_off = jnp.arange(SEL_LEN)
    jblk = jnp.arange(n_slc)

    def block_fn(blk):
        q0 = blk * Q_BLOCK
        qb = lax.dynamic_slice_in_dim(qg, q0, Q_BLOCK, axis=3)
        gb = lax.dynamic_slice_in_dim(gates, q0, Q_BLOCK, axis=3)
        t = q0 + jnp.arange(Q_BLOCK)
        p_c = masked_softmax(jnp.einsum('bghqd,bgcd->bghqc', qb, kc),
                             cmp_end[None, :] <= t[:, None])
        o_c = jnp.einsum('bghqc,bgcd->bghqd', p_c.astype(vc.dtype), vc)
        imp = jnp.einsum('bghqc,cj->bgqj', p_c, overlap)
        cur = t // SEL_LEN
        causal_blk = jblk[None, :] <= cur[:, None]
        forced = (jblk[None, :] == 0) | (jblk[None, :] == cur[:, None]) | (jblk[None, :] == cur[:, None] - 1)
        imp = jnp.where(forced & causal_blk, FORCE_SCORE, imp)
        imp = jnp.where(causal_blk, imp, NEG)
        top_val, top_idx = lax.top_k(imp, n_top)
        tok_idx = top_idx[..., None] * SEL_LEN + sel_off
        tok_ok = (top_val > 0.5 * NEG)[..., None] & (tok_idx <= t[None, None, :, None, None])
        flat_idx = tok_idx.reshape(bsz, G, Q_BLOCK * n_top * SEL_LEN)
        k_sel = ks_g[bi, gi, flat_idx].reshape(bsz, G, Q_BLOCK, n_top * SEL_LEN, HD)
        v_sel = vs_g[bi, gi, flat_idx].reshape(bsz, G, Q_BLOCK, n_top * SEL_LEN, HD)
        p_s = masked_softmax(jnp.einsum('bghqd,bgqkd->bghqk', qb, k_sel),
                             tok_ok.reshape(bsz, G, 1, Q_BLOCK, n_top * SEL_LEN))
        o_s = jnp.einsum('bghqk,bgqkd->bghqd', p_s.astype(v_sel.dtype), v_sel)
        k_w = lax.dynamic_slice_in_dim(kw_pad, q0, WINDOW + Q_BLOCK, axis=2)
        v_w = lax.dynamic_slice_in_dim(vw_pad, q0, WINDOW + Q_BLOCK, axis=2)
        s_pos = q0 - WINDOW + jnp.arange(WINDOW + Q_BLOCK)
        m_w = (s_pos[None, :] <= t[:, None]) & (s_pos[None, :] > t[:, None] - WINDOW) & (s_pos[None, :] >= 0)
        p_w = masked_softmax(jnp.einsum('bghqd,bgkd->bghqk', qb, k_w), m_w)
        o_w = jnp.einsum('bghqk,bgkd->bghqd', p_w.astype(v_w.dtype), v_w)
        return gb[..., 0:1] * o_c + gb[..., 1:2] * o_s + gb[..., 2:3] * o_w

    out = lax.map(block_fn, jnp.arange(s // Q_BLOCK))
    return out.transpose(1, 0, 4, 2, 3, 5).reshape(bsz, s, B_Q_W)

def second_inputs(seed: int = 0) -> dict:
    key = jax.random.key(seed)
    ks = jax.random.split(key, 20)
    f32 = jnp.float32

    def nrm(k, shape, scale):
        return jax.random.normal(k, shape, f32) * scale

    L = DEPTH_2
    x = jax.random.normal(ks[0], (BATCH, SEQ, D_MODEL), f32)
    offsets = jax.random.randint(ks[1], (BATCH, 1), 0, 2048, dtype=jnp.int32)
    positions = (offsets + jnp.arange(SEQ, dtype=jnp.int32)[None, :]).astype(jnp.int32)
    return {
        "x": x,
        "positions": positions,
        "norm1_g": 1.0 + nrm(ks[2], (L, D_MODEL), 0.02),
        "w_in": nrm(ks[3], (L, D_MODEL, N_IN), D_MODEL ** -0.5),
        "lb_param": nrm(ks[4], (L + 1, A_QK_W), 0.1),
        "hgrn_norm_g": 1.0 + nrm(ks[5], (L, A_DV), 0.02),
        "cmp_pe_k": nrm(ks[6], (L, CMP_LEN, B_HEAD_DIM), 0.1),
        "cmp_pe_v": nrm(ks[7], (L, CMP_LEN, B_HEAD_DIM), 0.1),
        "cmp_w1_k": nrm(ks[8], (L, CMP_LEN * B_HEAD_DIM, CMP_HIDDEN), (CMP_LEN * B_HEAD_DIM) ** -0.5),
        "cmp_w2_k": nrm(ks[9], (L, CMP_HIDDEN, B_HEAD_DIM), CMP_HIDDEN ** -0.5),
        "cmp_w1_v": nrm(ks[10], (L, CMP_LEN * B_HEAD_DIM, CMP_HIDDEN), (CMP_LEN * B_HEAD_DIM) ** -0.5),
        "cmp_w2_v": nrm(ks[11], (L, CMP_HIDDEN, B_HEAD_DIM), CMP_HIDDEN ** -0.5),
        "w_br_a": nrm(ks[12], (L, A_V_W, D_MODEL), A_V_W ** -0.5),
        "w_br_b": nrm(ks[13], (L, B_Q_W, D_MODEL), B_Q_W ** -0.5),
        "w_out": nrm(ks[14], (L, D_MODEL, D_MODEL), D_MODEL ** -0.5),
        "norm2_g": 1.0 + nrm(ks[15], (L, D_MODEL), 0.02),
        "w_ff1": nrm(ks[16], (L, D_MODEL, D_FF_2), D_MODEL ** -0.5),
        "w_ff2": nrm(ks[17], (L, D_FF_2, D_MODEL), D_FF_2 ** -0.5),
        "final_g": 1.0 + nrm(ks[18], (D_MODEL,), 0.02),
    }

def second_block(x, positions, norm1_g, w_in, lb_param, hgrn_norm_g, cmp_pe_k, cmp_pe_v,
              cmp_w1_k, cmp_w2_k, cmp_w1_v, cmp_w2_v, w_br_a, w_br_b, w_out,
              norm2_g, w_ff1, w_ff2, final_g):
    lb_all = jnp.cumsum(jax.nn.softmax(lb_param.astype(jnp.float32), axis=0), axis=0)
    h = x
    for l in range(DEPTH_2):
        xn = rmsnorm(h, norm1_g[l])
        proj = xn @ w_in[l]
        a_q, a_f, a_i, a_g, b_q, b_kv, b_gate, m_gate = jnp.split(proj, SPLIT_POINTS, axis=-1)
        kc, vc, ks_, vs_, kw_, vw_ = jnp.split(b_kv, 6, axis=-1)
        y_a = hgrn2_mixer(a_q, a_f, a_i, a_g, lb_all[l], hgrn_norm_g[l])
        y_b = nsa_mixer(b_q, kc, vc, ks_, vs_, kw_, vw_, b_gate, positions,
                        cmp_pe_k[l], cmp_pe_v[l], cmp_w1_k[l], cmp_w2_k[l], cmp_w1_v[l], cmp_w2_v[l])
        g_a, g_b = jnp.split(jax.nn.sigmoid(m_gate), 2, axis=-1)
        merged = g_a * (y_a @ w_br_a[l]) + g_b * (y_b @ w_br_b[l])
        h = h + merged @ w_out[l]
        hn = rmsnorm(h, norm2_g[l])
        h = h + jnp.square(jax.nn.relu(hn @ w_ff1[l])) @ w_ff2[l]
    return rmsnorm(h, final_g)


def setup_inputs(seed=0):
    out = dict(first_inputs(seed))
    for name, value in second_inputs(seed + 1).items():
        if name != "x":
            out[name + "_2"] = value
    return out


def reference(
    x, g_norm, w_ffn_gate, w_ffn_up, w_ffn_down, w_conv_in, w_conv, w_conv_out, g_kv, w_kv, w_q,
    lambda_q1, lambda_k1, lambda_q2, lambda_k2, g_subln, w_o, positions_2, norm1_g_2, w_in_2,
    lb_param_2, hgrn_norm_g_2, cmp_pe_k_2, cmp_pe_v_2, cmp_w1_k_2, cmp_w2_k_2, cmp_w1_v_2,
    cmp_w2_v_2, w_br_a_2, w_br_b_2, w_out_2, norm2_g_2, w_ff1_2, w_ff2_2, final_g_2,
):
    x = first_block(
        x, g_norm, w_ffn_gate, w_ffn_up, w_ffn_down, w_conv_in, w_conv, w_conv_out, g_kv, w_kv,
        w_q, lambda_q1, lambda_k1, lambda_q2, lambda_k2, g_subln, w_o,
    )
    return second_block(
        x, positions_2, norm1_g_2, w_in_2, lb_param_2, hgrn_norm_g_2, cmp_pe_k_2, cmp_pe_v_2,
        cmp_w1_k_2, cmp_w2_k_2, cmp_w1_v_2, cmp_w2_v_2, w_br_a_2, w_br_b_2, w_out_2, norm2_g_2,
        w_ff1_2, w_ff2_2, final_g_2,
    )


_drawn_inputs = setup_inputs


def setup_inputs(seed=0):
    import zlib

    import numpy as np

    out = dict(_drawn_inputs(seed))
    spreads = {}
    factors = {'g_kv': 3.3,
     'g_subln': 4.71,
     'norm1_g_2': 7.3,
     'lb_param_2': 4.169,
     'hgrn_norm_g_2': 8.0,
     'cmp_pe_k_2': 23.133,
     'cmp_pe_v_2': 50.597,
     'cmp_w1_k_2': 3.743,
     'cmp_w2_k_2': 3.594,
     'norm2_g_2': 16.845,
     'final_g_2': 7.725}
    for name, (base, spread) in spreads.items():
        noise = np.random.default_rng([zlib.crc32(name.encode()), seed]).standard_normal(out[name].shape)
        drawn = base * np.exp(spread * noise) if base else spread * noise
        out[name] = __import__('jax').numpy.asarray(drawn.astype(out[name].dtype))
    for name, factor in factors.items():
        out[name] = (out[name] * factor).astype(out[name].dtype)
    return out
```

```python
import math
from contextlib import ExitStack

import numpy as np
import concourse.bass as bass
from concourse import mybir
from concourse.alu_op_type import AluOpType as ALU

F32 = mybir.dt.float32
F32R = mybir.dt.float32r
I32 = mybir.dt.int32
ACT = mybir.ActivationFunctionType
AX = mybir.AxisListType

P = 128
D = 1024
KT = D // P
TT = 2
S = TT * P
FG = 256
D_FF = 2816
STEPS = D_FF // FG
D_FF2 = 4 * D
STEPS2 = D_FF2 // 512
EPS = 1e-6
LAMBDA_INIT = 0.8 - 0.6 * math.exp(-0.3)
NEG = -1e30
N_IN = 5400
HGRN_H = 4
CH = 64
NCMP = (S - 32) // 16 + 1
C_Q, C_F, C_V, C_G, C_BQ = 0, 512, 1024, 1536, 2048
C_KC, C_VC, C_KS, C_VS, C_KW, C_VW = (2560 + 128 * i for i in range(6))
C_GATE, C_MG = 3328, 3352
ROT = 8
R_GKV, R_N1, R_N2, R_LB = 96, 104, 112, 120
R_PEK, R_PEV, R_SUB, R_HG, N_SM2 = 24, 40, 56, 57, 58


class Entry:

    def __init__(self, slot, raw_before, split_before, kt, cols, split, pieces, step):
        self.step = step
        self.slot, self.raw_before, self.split_before = slot, raw_before, split_before
        self.kt, self.cols, self.split, self.pieces = kt, cols, split, pieces


class Stream:

    def __init__(self):
        self.entries, self.raw, self.split = [], [0] * 4, [0] * 4
        self.segment, self.allow = {}, {}

    def start(self, name, allow):
        self.segment[name], self.allow[name] = len(self.entries), allow

    def add(self, slot, kt, cols, pieces, split=True, step=0):
        self.entries.append(Entry(slot, self.raw[slot], self.split[slot], kt, cols, split, pieces, step))
        self.raw[slot] += 1
        self.split[slot] += split


def tiled(w):
    return w.rearrange("(k p) n -> p k n", p=P)


def plan(a):
    st = Stream()
    pair = [0]

    def two(src, kt_each, n_pieces=2):
        h = kt_each // n_pieces
        return [(slice(i * h, (i + 1) * h), None, src[:, i * h:(i + 1) * h, :]) for i in range(n_pieces)]

    def linear(name, w, allow=4):
        st.start(name, allow)
        w, n = tiled(w), w.shape[1]
        for c in range(0, n, 512):
            m = min(512, n - c)
            for half in range(2):
                st.add(pair[0] * 2 + half, 4, m, two(w[:, 4 * half:4 * half + 4, c:c + m], 4))
            pair[0] ^= 1

    def ffn(name, layer, which):
        st.start(name, 2)
        gate, up = tiled(a["w_ffn_gate"][layer, which]), tiled(a["w_ffn_up"][layer, which])
        down = tiled(a["w_ffn_down"][layer, which])

        def first(g):
            for half in range(2):
                ks = slice(4 * half, 4 * half + 4)
                st.add(half, 4, 512, [
                    (slice(0, 4), slice(0, FG), lambda i, ks=ks: gate[:, ks, bass.ds(i * FG, FG)]),
                    (slice(0, 4), slice(FG, 512), lambda i, ks=ks: up[:, ks, bass.ds(i * FG, FG)])], step=g)

        def second(g):
            st.add(2 if g < STEPS - 1 else 3, 2, 1024, [
                (slice(k, k + 1), None, lambda i, k=k: down[:, bass.ds(2 * i + k, 1), :]) for k in range(2)], step=g)

        first(0)
        for g in range(1, STEPS):
            first(g)
            second(g - 1)
        second(STEPS - 1)
        pair[0] = 0

    def ff(name):
        st.start(name, 2)
        w1, w2 = tiled(a["w_ff1_2"][0]), tiled(a["w_ff2_2"][0])

        def first(g):
            for half in range(2):
                st.add(half, 4, 512, [
                    (slice(k, k + 2), None, lambda i, k=k, half=half: w1[:, 4 * half + k:4 * half + k + 2, bass.ds(i * 512, 512)])
                    for k in (0, 2)], step=g)

        def second(g):
            for half in range(2):
                st.add(2 + half, 2, 1024, [
                    (slice(k, k + 1), None, lambda i, k=k, half=half: w2[:, bass.ds(4 * i + 2 * half + k, 1), :])
                    for k in range(2)], step=g)

        first(0)
        for g in range(1, STEPS2):
            first(g)
            second(g - 1)
        second(STEPS2 - 1)

    ffn("ffn0", 0, 0)
    linear("conv_in", a["w_conv_in"][0])
    linear("conv_out", a["w_conv_out"][0])
    ffn("ffn1", 0, 1)
    linear("kv", a["w_kv"])
    ffn("ffn2", 1, 0)
    linear("q", a["w_q"][0])
    linear("o", a["w_o"][0])
    ffn("ffn3", 1, 1)
    linear("w_in", a["w_in_2"][0])
    st.start("cmp", 4)
    for i, name in enumerate(("cmp_w1_k_2", "cmp_w1_v_2")):
        w = tiled(a[name][0])
        for half in range(2):
            st.add(pair[0] * 2 + half, 8, 256, two(w[:, 8 * half:8 * half + 8, :], 8), split=False)
        pair[0] ^= 1
    st.start("branch", 4)
    br = [tiled(a["w_br_a_2"][0]), tiled(a["w_br_b_2"][0])]
    for nn in range(2):
        for i in range(2):
            st.add(pair[0] * 2 + i, 4, 512, two(br[i][:, :, 512 * nn:512 * nn + 512], 4))
        pair[0] ^= 1
    linear("w_out", a["w_out_2"][0])
    ff("ff")
    st.start("end", 0)
    return st


def two_blocks(nc, a, out, stop=None):
    ctx = ExitStack()
    with ctx:
        def sb(name, shape, dt=F32):
            return ctx.enter_context(nc.sbuf_tensor(name, shape, dt))

        def sem(name):
            return ctx.enter_context(nc.semaphore(name))

        st = plan(a)
        ent, seg = st.entries, st.segment

        raw = [sb(f"raw{i}", [P, 2048]) for i in range(4)]
        whi = [sb(f"whi{i}", [P, 2048], F32R) for i in range(4)]
        wlo = [sb(f"wlo{i}", [P, 2048], F32R) for i in range(4)]
        x = sb("x", [P, TT, D])
        xh = sb("xh", [P, KT, S], F32R)
        xl = sb("xl", [P, KT, S], F32R)
        hth = sb("hth", [P, 4, S], F32R)
        htl = sb("htl", [P, 4, S], F32R)
        hid = sb("hid", [P, TT, 512])
        sg = sb("sg", [P, TT, 512])
        proj = sb("proj", [P, TT * N_IN])
        gain = sb("gain", [P, 2, D])
        tmp = sb("tmp", [P, TT, D])
        junk = sb("junk", [P, D])
        ident = sb("ident", [P, P])
        rows1 = sg[:, 0, 0:P]
        rows2 = sg[0:N_SM2, 1, 0:P]
        col1 = sb("col1", [P, P])
        col2 = sb("col2", [P, N_SM2])
        ssq = sb("ssq", [P, 40])
        msq = sb("msq", [P, 40])
        rs = sb("rs", [P, 40])
        r8 = sb("r8", [P, TT])
        nhalf = sb("nhalf", [P, 16])
        GU = ctx.enter_context(nc.psum_tensor("GU", [P, 2, 512], F32))
        DD = ctx.enter_context(nc.psum_tensor("DD", [P, 4, 512], F32))
        TB = ctx.enter_context(nc.psum_tensor("TB", [P, 2, 512], F32))

        loaded = [sem(f"loaded{i}") for i in range(4)]
        hi_done = [sem(f"hi_done{i}") for i in range(4)]
        lo_done = [sem(f"lo_done{i}") for i in range(4)]
        used = [sem(f"used{i}") for i in range(4)]
        gu_ready = sem("gu_ready")
        gu_used = [sem(f"gu_used{i}") for i in range(2)]
        d_ready = sem("d_ready")
        d_used = [sem(f"d_used{i}") for i in range(2)]
        t_ready = [sem(f"t_ready{i}") for i in range(2)]
        t_used = [sem(f"t_used{i}") for i in range(2)]
        xh_done = sem("xh_done")
        hth_done = [sem(f"hth_done{i}") for i in range(2)]
        sg_done = [sem(f"sg_done{i}") for i in range(2)]
        d_part = sem("d_part")
        h_ready = [sem(f"h_ready{i}") for i in range(2)]
        x_ready = sem("x_ready")
        x_loaded = sem("x_loaded")
        small_loaded = sem("small_loaded")
        gain_loaded = [sem("gain_loaded0"), sem("gain_loaded1")]
        ssq_ready = sem("ssq_ready")
        rs_ready = sem("rs_ready")
        act_chain, dve_chain, pool_chain = sem("act_chain"), sem("dve_chain"), sem("pool_chain")
        const_ready = sem("const_ready")
        cols_t = sem("cols_t")
        cols_ready = sem("cols_ready")
        out_ready, out_done = sem("out_ready"), sem("out_done")

        def view(buf, e):
            return buf[:, 0:e.kt * e.cols].rearrange("p (k n) -> p k n", k=e.kt)

        NORMS = ["pre0", "post0", "pre1", "post1", "pre2", "post2", "pre3", "post3", "pre5", "post4",
                 "pre6", "post5", "pre7", "pre8", "final"]
        ncol = {name: 2 * i for i, name in enumerate(NORMS)}
        ncol["pre4"] = ncol["pre3"]
        GAIN = [a["g_norm"][l, j:j + 1, :] for l in range(2) for j in (1, 3, 5)] + [a["final_g_2"].unsqueeze(0)]
        HALF = [0.5, 1.0, 0.5, 0.5, 1.0, 0.5]

        def rcol(name, tt):
            c = ncol[name] + tt
            return rs[:, c:c + 1]

        def gcols(first):
            return lambda k: col1[:, first + k:first + k + 1]

        PRE = {"pre0": gcols(0), "pre1": gcols(16), "pre2": gcols(32), "pre3": gcols(R_GKV),
               "pre4": gcols(48), "pre5": gcols(64), "pre6": gcols(80), "pre7": gcols(R_N1),
               "pre8": gcols(R_N2)}

        def P3(lo, n, base=0, width=N_IN):
            return proj[:, base:base + TT * width].rearrange("p (t n) -> p t n", t=TT)[:, :, lo:lo + n]

        V_AT, KTOK_AT = 0, 2048
        KT_AT, QT_AT, O_AT = 4096, 6144, 8192
        vtok = proj[:, V_AT:V_AT + 2048].rearrange("p (t n) -> p t n", t=TT)
        ktok = proj[:, KTOK_AT:KTOK_AT + 2048].rearrange("p (t n) -> p t n", t=TT)
        kT = proj[:, KT_AT:KT_AT + 2048].rearrange("p (h n) -> p h n", h=8)
        qT = proj[:, QT_AT:QT_AT + 2048].rearrange("p (h n) -> p h n", h=8)
        otok = proj[:, O_AT:O_AT + 2048].rearrange("p (t n) -> p t n", t=TT)

        class Places:

            def __init__(self):
                self.next, self.gu, self.d, self.t, self.xh, self.hth = 0, 0, 0, [0, 0], 0, 0
                self.d0, self.x, self.h = 0, 0, 0
                self.gu0 = 0

        def ffn_shape(name):
            return (STEPS2, 2) if name == "ff" else (STEPS, 1)

        SMALL_LOADS = 10
        small = sb("small", [P, 1056])
        mask3 = sb("mask3", [P, 3 * P])
        sm = sb("sm", [P, 2, 2, 3 * P])
        at = sb("at", [P, 2, 6 * P])
        psc = sb("psc", [P, 2, 3 * P])
        lamv = small[:, 0:256].rearrange("p (i d) -> p i d", i=4)
        nmx = small[:, 256:264].rearrange("p (b c q) -> p b c q", b=2, c=2)
        den = small[:, 264:272].rearrange("p (b c q) -> p b c q", b=2, c=2)
        rden = small[:, 272:280].rearrange("p (b c q) -> p b c q", b=2, c=2)
        rl = small[:, 280:284].rearrange("p (b q) -> p b q", b=2)
        nlam = small[:, 284:285]
        lsum = small[:, 286:288]
        lexp = small[:, 288:290]
        gsub = small[:, 290:291]
        oss, omsq, ro = small[:, 296:312], small[:, 312:328], small[:, 328:344]
        flat = tmp[:, :, :].rearrange("p t n -> p (t n)")
        cpad = flat[:, 0:516].rearrange("p (b n) -> p b n", b=2)
        zaccs = [flat[:, 516:772], flat[:, 1284:1540]]
        zb = flat[:, 772:1284].rearrange("p (b n) -> p b n", b=2)
        cu_ready, cu_copied, conv_split = sem("cu_ready"), sem("cu_copied"), sem("conv_split")
        r8_ready, lam_loaded, lam_sums, lam_exp = sem("r8_ready"), sem("lam_loaded"), sem("lam_sums"), sem("lam_exp")
        sc_ready, sc_used, mx_ready, exp_done = sem("sc_ready"), sem("sc_used"), sem("mx_ready"), sem("exp_done")
        a_ready, pv_ready, pv_used = sem("a_ready"), sem("pv_ready"), sem("pv_used")
        oss_ready, ro_ready, o_ready = sem("oss_ready"), sem("ro_ready"), sem("o_ready")
        gsub_ready = sem("gsub_ready")

        def kv_dst(g, t):
            return (ktok if g < 2 else vtok)[:, t, (g % 2) * 512:(g % 2) * 512 + 512]

        def keys(qi):
            return slice(0, P) if qi == 0 else slice(P, 3 * P)


        cst = sb("cst", [P, 3 * P])
        posi = sb("posi", [P, TT], I32)
        coef, m64 = cst[:, 0:S], cst[:, S:3 * P]

        def s_(lo_, n_):
            return small[:, lo_:lo_ + n_]

        def heads4(t_):
            return t_.rearrange("p (h n) -> p h n", h=HGRN_H)

        lbt, lbe, lb, omlb = s_(344, 8), s_(352, 8), s_(360, 4), s_(364, 4)
        lbs, bl = s_(368, 4), s_(372, 16)
        hss, hms, hr = s_(388, 8), s_(396, 8), s_(404, 8)
        w2k = s_(412, 128).rearrange("p (h d) -> p h d", h=2)
        w2v = s_(540, 128).rearrange("p (h d) -> p h d", h=2)
        posf, ang = s_(668, 2), s_(672, 16)
        red, turns, trig = s_(688, 32), s_(720, 32), s_(752, 32)
        g1k = s_(784, 60).rearrange("p (h n) -> p h n", h=2)
        kcT, cmask, cneg = s_(904, 30), s_(934, 30), s_(964, 30)
        bdiag, invf, cmx, cden, wgt = s_(994, 8), s_(1002, 8), s_(1010, 16), s_(1026, 16), s_(1042, 8)
        g0, g1_ = gain[:, 0, :], gain[:, 1, :]
        hq, hf = hid[:, :, :].rearrange("p t n -> p (t n)"), sg[:, :, :].rearrange("p t n -> p (t n)")
        hk, he, hx, kltok = tmp[:, 0, :], tmp[:, 1, :], g0, junk[:, :]
        states = sm[:, :, :, :].rearrange("p a b n -> p (a b n)").rearrange("p (s n) -> p s n", s=3)
        amask = at[:, :, :].rearrange("p a n -> p (a n)")[:, 0:1024].rearrange("p (t n) -> p t n", t=TT)
        ya = P3(C_Q, 512)
        kc2, vc2 = (g0[:, i * 512:(i + 1) * 512].rearrange("p (g n) -> p g n", g=2) for i in range(2))
        ksT, kwT = (g1_[:, i * 512:(i + 1) * 512].rearrange("p (g n) -> p g n", g=2) for i in range(2))
        ff_k, ff_v = (hf[:, i * 480:(i + 1) * 480].rearrange("p (k g c) -> p k g c", k=16, g=2) for i in range(2))
        yb = hid[:, :, :]
        vbd = junk[0:120, 0:512]
        w2kk = junk[:, 512:768].rearrange("p (h u d) -> p h u d", h=2, u=2)
        g1x = junk[:, 768:1008].rearrange("p (h g e c) -> p h g e c", h=2, g=2, e=4)
        kd = flat.rearrange("p (i t g u d) -> p i t g u d", i=4, t=TT, g=2, u=2)
        pflat = psc[:, :, :].rearrange("p b n -> p (b n)")
        csc, pc, pcT = pflat[:, 0:240], pflat[:, 240:480], pflat[0:120, 480:736]
        merged = tmp[:, :, :]
        gel = at[0:2 * NCMP, :, 0:S]
        gate_cols = P3(C_GATE, 24)

        def qT2(j, lo_, n_):
            return P3(C_F, 512)[:, j // 2, (j % 2) * S + lo_:(j % 2) * S + lo_ + n_]

        kd_copied = sem("kd_copied")
        const2 = sem("const2")
        mix_loaded = sem("mix_loaded")
        gates_ready, lbt_ready, lbe_ready = sem("gates_ready"), sem("lbt_ready"), sem("lbe_ready")
        sf_ready, f_ready, lf_ready, b_ready, e_ready = (sem(x_) for x_ in ("sf_ready", "f_ready", "lf_ready", "b_ready", "e_ready"))
        bd_ready, el_ready, kd_ready, kl_ready = (sem(x_) for x_ in ("bd_ready", "el_ready", "kd_ready", "kl_ready"))
        attn_ready, am_ready, kv_ready, st_ready = (sem(x_) for x_ in ("attn_ready", "am_ready", "kv_ready", "st_ready"))
        ho_ready, ho_copied, hss_ready, hr_ready, ya_ready = (sem(x_) for x_ in ("ho_ready", "ho_copied", "hss_ready", "hr_ready", "ya_ready"))
        red_ready, trig_ready, rope_ready, ffk_ready = (sem(x_) for x_ in ("red_ready", "trig_ready", "rope_ready", "ffk_ready"))
        gelu_ready, cmp_ready, kcT_ready, vbd_ready = (sem(x_) for x_ in ("gelu_ready", "cmp_ready", "kcT_ready", "vbd_ready"))
        csc_ready, cmx_ready, cexp_ready, pc_ready = (sem(x_) for x_ in ("csc_ready", "cmx_ready", "cexp_ready", "pc_ready"))
        oc_ready, yb_ready, br_ready, br_used, merged_ready = (sem(x_) for x_ in ("oc_ready", "yb_ready", "br_ready", "br_used", "merged_ready"))
        UNITS = 8

        def unit(v):
            br, j = v // 4, v % 4
            g = j // 2
            return br, j, g, (ksT, kwT)[br], P3((C_VS, C_VW)[br] + 64 * g, 64)


        block = ctx.enter_context(nc.Block())

        @block.sync
        def _(sp):
            at = [0]

            def load(e, d=0):
                if e.raw_before or not isinstance(d, int):
                    sp.wait_ge(lo_done[e.slot], d + e.raw_before)
                for ks, cs, src in e.pieces:
                    v = view(raw[e.slot], e)[:, ks, :] if cs is None else view(raw[e.slot], e)[:, ks, cs]
                    sp.dma_start(v, src(d + e.step) if callable(src) else src).then_inc(loaded[e.slot], 16)

            def load_next(n):
                for _ in range(n):
                    load(ent[at[0]])
                    at[0] += 1

            def load_gain(i):
                if i >= 2:
                    sp.wait_ge(x_ready, 4 * (i - 1))
                sp.dma_start(gain[:, i % 2, :], GAIN[i].broadcast_to([P, D])).then_inc(gain_loaded[i % 2], 16)

            def ffn_loads(name, done=0):
                steps, nd = ffn_shape(name)
                per = 2 + nd
                load_next(4 + per - done)
                with sp.Fori(0, steps - 3) as i:
                    for e in ent[at[0]:at[0] + per]:
                        load(e, i)
                at[0] += per * (steps - 3)
                load_next(2 * nd)

            sp.dma_start(x[:, :, :], a["x"][0].rearrange("(t p) d -> p t d", p=P)).then_inc(x_loaded, 16)
            load_next(4)
            load_gain(0)
            load_gain(1)
            for i, name in enumerate(("lambda_q1", "lambda_k1", "lambda_q2", "lambda_k2")):
                sp.dma_start(lamv[:, i, :], a[name].broadcast_to([P, 64])).then_inc(lam_loaded, 16)
            with nc.allow_non_contiguous_dma(reason="256 positions"):
                sp.dma_start(posi[:, :], a["positions_2"][0].rearrange("(t p) -> p t", p=P)).then_inc(mix_loaded, 16)
            for t_, name in ((w2k, "cmp_w2_k_2"), (w2v, "cmp_w2_v_2")):
                sp.dma_start(t_, a[name][0].rearrange("(h p) d -> p h d", p=P)).then_inc(mix_loaded, 16)
            ffn_loads("ffn0", done=4)
            load_next(seg["ffn1"] - at[0])
            load_gain(2)
            ffn_loads("ffn1")
            load_gain(3)
            load_next(seg["ffn2"] - at[0])
            ffn_loads("ffn2")
            load_gain(4)
            load_next(seg["ffn3"] - at[0])
            load_gain(5)
            ffn_loads("ffn3")
            load_next(seg["ff"] - at[0])
            ffn_loads("ff")
            sp.wait_ge(x_ready, 28)
            load_gain(6)
            assert at[0] == len(ent)
            sp.wait_ge(out_ready, 2)
            sp.dma_start(out[0].rearrange("(t p) d -> p t d", p=P), tmp[:, :, :]).then_inc(out_done, 16)
            sp.wait_ge(out_done, 16)

        @block.tensor
        def _(pe):
            n = Places()
            xt_waits = [0]

            def mm3(dst, h, l, w_h, w_l, start, stop):
                pe.matmul(dst, h, w_h, start=start, stop=False)
                pe.matmul(dst, h, w_l, start=False, stop=False)
                return pe.matmul(dst, l, w_h, start=False, stop=stop)

            def x_half(dst, e, half, first_k, last, d=0, done=None, read=None):
                s, m = e.slot, e.cols
                take_xt(first_k)
                pe.wait_ge(lo_done[s], d + e.raw_before + 1)
                wh, wl = view(whi[s], e), view(wlo[s], e)
                order = [(k, t) for t in range(TT) for k in range(4)] if last else \
                        [(k, t) for k in range(4) for t in range(TT)]
                for i, (k, t) in enumerate(order):
                    kk, ts = first_k + k, slice(t * P, (t + 1) * P)
                    if read and i < 2 and read[1]:
                        pe.wait_ge(read[0][t], read[1])
                    if t == 0 and kk == 2:
                        take_xt(kk)
                    mm = mm3(dst[t][:, 0:m], xh[:, kk, ts], xl[:, kk, ts], wh[:, k, :], wl[:, k, :],
                             start=(half == 0 and k == 0), stop=(last and k == 3))
                    if last and i == 3:
                        mm.then_inc(done, 1)
                mm.then_inc(used[s], 1)

            def bank_transposes(bank, blocks, rows=P):
                if n.t[bank]:
                    pe.wait_ge(t_used[bank], n.t[bank])
                for c, src in blocks:
                    r, m = src.shape[0], src.free_size()
                    mm = pe.transpose(TB[0:m, bank, c:c + r], src, ident[0:r, 0:r])
                mm.then_inc(t_ready[bank], 1)
                n.t[bank] += 1

            pending = {}

            def fill(src, b):
                bank_transposes(b % 2, [((2 * j + t) * P, src[:, t, (2 * b + j) * P:(2 * b + j + 1) * P])
                                        for j in range(2) for t in range(TT)])

            def prep(src, kts=range(KT), defer=False):
                for b in range(len(kts) // 2):
                    if not (defer and b >= 2):
                        fill(src, b)
                if defer:
                    pending.update({0: [(src, 2, 0)], 2: [(src, 3, 0)], 4: []})

            def take_xt(at):
                if at not in pending:
                    return
                if at < 4:
                    pe.wait_ge(t_used[at // 2], n.t[at // 2])
                for src, b, count in pending.pop(at):
                    if count:
                        pe.wait_ge(x_ready if src is x else o_ready if src is otok else br_used, count)
                    fill(src, b)
                if at == 4:
                    wait_xt()

            def wait_xt():
                pe.wait_ge(t_used[0], n.t[0])
                pe.wait_ge(t_used[1], n.t[1])

            def prep_x():
                n.x += 1
                if n.x > 1:
                    pe.wait_ge(x_ready, 4 * (n.x - 1) - 1)
                else:
                    pe.wait_ge(x_loaded, 16)
                    pe.wait_ge(const_ready, 1)
                    pe.wait_ge(cols_ready, 2)
                prep(x, defer=True)
                if n.x > 1:
                    pending[0] = [(x, 2, 4 * (n.x - 1))]

            def wait_d():
                for t in range(TT):
                    if n.d:
                        pe.wait_ge(d_used[t], n.d)
                n.d += 1

            def group(which):
                e0, e1 = ent[n.next:n.next + 2]
                n.next += 2
                if which == "gu":
                    read, dst, done = (gu_used, n.gu), [GU[:, 0, :], GU[:, 1, :]], gu_ready
                    n.gu += 1
                else:
                    read, dst, done = (d_used, n.d), [DD[:, 0, :], DD[:, 2, :]], d_ready
                    n.d += 1
                x_half(dst, e0, 0, 0, False, read=read)
                x_half(dst, e1, 1, 4, True, done=done)

            def full_to_dd():
                wait_d()
                for nn in range(2):
                    e0, e1 = ent[n.next:n.next + 2]
                    n.next += 2
                    dst = [DD[:, nn, :], DD[:, 2 + nn, :]]
                    x_half(dst, e0, 0, 0, False)
                    x_half(dst, e1, 1, 4, True, done=d_ready if nn else d_part)

            def ffn(name):
                steps, nd = ffn_shape(name)
                per, base, gu0 = 2 + nd, n.next, n.gu
                t0 = [v + bool(pending) for v in n.t]
                sq0 = n.h
                gu_banks = [GU[:, 0, :], GU[:, 1, :]]

                def hidden_transposes(g, d):
                    for t in range(TT):
                        if nd == 1:
                            pe.wait_ge(gu_used[t], d + gu0 + g + 1)
                        else:
                            pe.wait_ge(h_ready[t], d + sq0 + g + 1)
                    for b in range(nd):
                        for j in range(2):
                            for t in range(TT):
                                mm = pe.transpose(TB[:, b, (2 * j + t) * P:(2 * j + t + 1) * P],
                                                  hid[:, t, (2 * b + j) * P:(2 * b + j + 1) * P], ident[:, :])
                        mm.then_inc(t_ready[b], 1)

                def down(g, es, d, start, stop):
                    for b, e in enumerate(es):
                        pe.wait_ge(t_used[b], d + t0[b] + g + 1)
                        pe.wait_ge(lo_done[e.slot], d + e.raw_before + 1)
                        wh, wl = view(whi[e.slot], e), view(wlo[e.slot], e)
                        last = stop and b == nd - 1
                        order = [(k, t) for t in range(TT) for k in range(2)] if last else \
                                [(k, t) for k in range(2) for t in range(TT)]
                        for i, (k, t) in enumerate(order):
                            ts = slice(t * P, (t + 1) * P)
                            for nn in range(2):
                                cs = slice(nn * 512, (nn + 1) * 512)
                                mm = mm3(DD[:, 2 * t + nn, :], hth[:, 2 * b + k, ts], htl[:, 2 * b + k, ts],
                                         wh[:, k, cs], wl[:, k, cs],
                                         start=(start and b == 0 and k == 0), stop=(last and k == 1))
                            if last and i == 1:
                                mm.then_inc(d_ready, 1)
                        mm.then_inc(used[e.slot], 1)

                def step(g, at, d=0, static=True):
                    es = ent[at:at + per]
                    if gu0 + g > 0:
                        for t in range(TT):
                            pe.wait_ge(gu_used[t], d + gu0 + g)
                    x_half(gu_banks, es[0], 0, 0, False, d=d)
                    if g:
                        hidden_transposes(g - 1, d)
                    x_half(gu_banks, es[1], 1, 4, True, d=d, done=gu_ready)
                    if g:
                        down(g - 1, es[2:], d, start=(static and g == 1), stop=False)

                if name == "ff":
                    n.d += 1
                else:
                    wait_d()
                step(0, base)
                step(1, base + 2)
                step(2, base + 2 + per)
                with pe.Fori(0, steps - 3) as i:
                    step(3, base + 2 + 2 * per, d=i, static=False)
                n.next = base + 2 + per * (steps - 1) + nd
                hidden_transposes(steps - 1, 0)
                down(steps - 1, ent[n.next - nd:n.next], 0, start=False, stop=True)
                n.gu = gu0 + steps
                for b in range(nd):
                    n.t[b] = t0[b] + steps
                if nd == 2:
                    n.h += steps

            def wait_results():
                for t in range(TT):
                    pe.wait_ge(gu_used[t], n.gu)
                    pe.wait_ge(d_used[t], n.d)

            def pe_conv():
                cu = P3(D, D, 0, 3 * D)
                bg = P3(0, D, 0, 3 * D)
                for k in range(KT):
                    if k % 4 == 0:
                        pe.wait_ge(cu_ready, k // 4 + 1)
                    ks = slice(k * P, (k + 1) * P)
                    bank_transposes(k % 2, [(t * P, cu[:, t, ks]) for t in range(TT)] +
                                    [(S + t * P, bg[:, t, ks]) for t in range(TT)])
                pe.wait_ge(conv_split, KT)

            def pe_attention():
                t_of = {}
                for u in range(-1, 10):
                    if u < 7:
                        w = u + 1
                        if w >= 2:
                            pe.wait_ge(sc_used, w - 1)
                        for c in range(2):
                            cs = slice(64 * c, 64 * c + 64)
                            for qi in range(TT):
                                mm = pe.matmul(DD[:, 2 * (w % 2) + c, keys(qi)], qT[cs, w, qi * P:(qi + 1) * P],
                                               kT[cs, w, 0:(qi + 1) * P], start=True, stop=True)
                        mm.then_inc(sc_ready, 1)
                    if 1 <= u < 9:
                        pe.wait_ge(a_ready, u)
                        b = (u - 1) % 2
                        bank_transposes(b, [(j * P, psc[:, b, j * P:(j + 1) * P]) for j in range(3)])
                        t_of[u - 1] = n.t[b]
                    if u >= 2:
                        h, b = u - 2, u % 2
                        pe.wait_ge(t_used[b], t_of[h])
                        if h >= 2:
                            pe.wait_ge(pv_used, h - 1)
                        hs = slice(h * P, (h + 1) * P)
                        pe.matmul(GU[:, b, 0:P], at[:, b, 0:P], vtok[:, 0, hs], start=True, stop=True)
                        pe.matmul(GU[:, b, P:2 * P], at[:, b, P:2 * P], vtok[:, 0, hs], start=True, stop=False)
                        pe.matmul(GU[:, b, P:2 * P], at[:, b, 2 * P:3 * P], vtok[:, 1, hs], start=False, stop=True)\
                            .then_inc(pv_ready, 1)


            def pe_mixers():
                group("gu")
                group("d")
                group("gu")
                for t in range(TT):
                    pe.wait_ge(gu_used[t], n.gu - 1)
                    pe.wait_ge(d_used[t], n.d)
                for c0 in (C_Q, C_F):
                    for b in range(2):
                        bank_transposes(b, [((2 * j + t) * P, P3(c0, 512)[:, t, (2 * b + j) * P:(2 * b + j + 1) * P])
                                            for j in range(2) for t in range(TT)])
                group("d")
                group("gu")
                for t in range(TT):
                    pe.wait_ge(d_used[t], n.d)
                pe.wait_ge(kd_ready, 2)
                for t in range(TT):
                    for h in range(HGRN_H):
                        cs = slice(t * P, (t + 1) * P)
                        mm = pe.matmul(DD[:, t, h * P:(h + 1) * P], heads4(hx)[:, h, cs], heads4(hq)[:, h, cs],
                                       start=True, stop=True)
                    mm.then_inc(attn_ready, 1)
                group("gu")
                pe.wait_ge(kl_ready, 1)
                for b in range(2):
                    bank_transposes(b, [((2 * j + t) * P, heads4(hk)[:, 2 * b + j, t * P:(t + 1) * P])
                                        for j in range(2) for t in range(TT)])
                group("gu")
                wait_xt()
                for i, bank in ((0, DD[:, 2, :]), (1, DD[:, 3, :]), (2, DD[:, 0, :])):
                    if i == 2:
                        pe.wait_ge(am_ready, 1)
                    t, rows = i // 2, slice(CH * (i % 2), CH * (i % 2) + CH)
                    for h in range(HGRN_H):
                        kc = (h // 2) * 512 + (2 * (h % 2) + t) * P
                        mm = pe.matmul(bank[:, h * P:(h + 1) * P], kltok[rows, kc:kc + P],
                                       P3(C_V, 512)[rows, t, h * P:(h + 1) * P], start=True, stop=True)
                    mm.then_inc(kv_ready, 1)
                group("gu")
                pe.wait_ge(st_ready, 3)
                for t in range(TT):
                    pe.wait_ge(am_ready, t + 1)
                    bank = DD[:, 3 - t, :]
                    for h in range(HGRN_H):
                        hs = slice(h * P, (h + 1) * P)
                        mm = pe.matmul(bank[:, hs], amask[:, t, hs], P3(C_V, 512)[:, t, hs], start=True, stop=False,
                                       skip_group_check=True)
                        for i in range(2 * t, 2 * t + 2):
                            if i:
                                r0 = CH * (i % 2)
                                mm = pe.matmul(bank[r0:r0 + CH, hs], heads4(hq)[:, h, i * CH:(i + 1) * CH],
                                               states[:, i - 1, hs], start=False, stop=True, skip_group_check=True)
                    mm.then_inc(ho_ready, 1)
                group("gu")
                pe.wait_ge(rope_ready, 1)
                for b in range(2):
                    bank_transposes(b, [((2 * j + t) * P, P3(C_BQ, 512)[:, t, (2 * b + j) * P:(2 * b + j + 1) * P])
                                        for j in range(2) for t in range(TT)])
                pe.wait_ge(kd_copied, 1)
                for i in range(4):
                    bank_transposes(i % 2, [((2 * g + t) * P, kd[:, i, t, g, :, :].rearrange("p u d -> p (u d)"))
                                            for g in range(2) for t in range(TT)])
                group("gu")
                for i, f_ in enumerate((ff_k, ff_v)):
                    es = ent[seg["cmp"] + 2 * i:seg["cmp"] + 2 * i + 2]
                    for e in es:
                        pe.wait_ge(loaded[e.slot], 32 * (e.raw_before + 1))
                    pe.wait_ge(ffk_ready, i + 1)
                    for k in range(16):
                        e = es[k // 8]
                        mm = pe.matmul(DD[0:2 * NCMP, i, 0:256], f_[:, k, :, :].rearrange("p g c -> p (g c)"),
                                       view(raw[e.slot], e)[:, k % 8, :], start=(k == 0), stop=(k == 15))
                        if k % 8 == 7:
                            mm.then_inc(lo_done[e.slot], 1)
                group("gu")
                n.next += 4
                for i in range(2):
                    pe.wait_ge(gelu_ready, i + 1)
                    bank_transposes(i, [(32 * hh, gel[:, i, hh * P:(hh + 1) * P]) for hh in range(2)])
                pe.wait_ge(ho_copied, 2)
                wait_xt()
                for hh in range(2):
                    mm = pe.matmul(DD[:, 2, 0:30], w2kk[:, hh, :, :].rearrange("p u d -> p (u d)"), g1k[:, hh, :],
                                   start=(hh == 0), stop=(hh == 1))
                mm.then_inc(cmp_ready, 1)
                for hh in range(2):
                    mm = pe.matmul(DD[0:120, 3, 0:64],
                                   g1x[:, hh, :, :, :].rearrange("p g e c -> p (g e c)"),
                                   w2v[:, hh, :], start=(hh == 0), stop=(hh == 1))
                mm.then_inc(cmp_ready, 1)
                pe.wait_ge(ya_ready, 1)
                prep(ya, range(4))
                pe.wait_ge(kcT_ready, 1)
                for t in range(TT):
                    pe.wait_ge(gu_used[t], n.gu)
                for i in range(2):
                    rows = slice(64 * i, 64 * i + 64)
                    for t in range(TT):
                        for j in range(4):
                            mm = pe.matmul(GU[:, i, (t * 4 + j) * 15:(t * 4 + j) * 15 + 15], qT2(j, t * P, P)[rows, :],
                                           kcT[rows, (j // 2) * 15:(j // 2) * 15 + 15], start=True, stop=True)
                mm.then_inc(csc_ready, 1)
                pe.wait_ge(pc_ready, 1)
                bank_transposes(0, [(t * P, pc[:, t * 120:(t + 1) * 120]) for t in range(TT)])
                pe.wait_ge(t_used[0], n.t[0])
                pe.wait_ge(vbd_ready, 1)
                for t in range(TT):
                    mm = pe.matmul(DD[:, t, :], pcT[:, t * P:(t + 1) * P], vbd, start=True, stop=True)
                mm.then_inc(oc_ready, 1)
                pe.wait_ge(yb_ready, 1)
                t_of = {}
                for u in range(UNITS + 2):
                    if u < UNITS:
                        br, j, g, kk, _ = unit(u)
                        pe.wait_ge(sc_used, 8 + u - 1 if u >= 2 else 8)
                        for c in range(2):
                            cs = slice(64 * c, 64 * c + 64)
                            for qi in range(TT):
                                mm = pe.matmul(DD[:, 2 * (u % 2) + c, keys(qi)], qT2(j, qi * P, P)[cs, :],
                                               kk[cs, g, 0:(qi + 1) * P], start=True, stop=True)
                        mm.then_inc(sc_ready, 1)
                    if 1 <= u < UNITS + 1:
                        pe.wait_ge(exp_done, 8 + u)
                        b = (u - 1) % 2
                        for i in range(2):
                            bank_transposes(i, [(q * P, sm[:, b, i, q * P:(q + 1) * P]) for q in range(3)])
                        t_of[u - 1] = list(n.t)
                    if u >= 2:
                        v, b = u - 2, u % 2
                        vals = unit(v)[4]
                        for i in range(2):
                            pe.wait_ge(t_used[i], t_of[v][i])
                        pe.wait_ge(pv_used, 8 + max(v - 1, 0))
                        for i in range(2):
                            lo_ = 3 * P * i
                            o0, o1 = (slice((2 * i + q) * 64, (2 * i + q) * 64 + 64) for q in range(2))
                            pe.matmul(GU[:, b, o0], at[:, b, lo_:lo_ + P], vals[:, 0, :], start=True, stop=True)
                            pe.matmul(GU[:, b, o1], at[:, b, lo_ + P:lo_ + 2 * P], vals[:, 0, :], start=True, stop=False)
                            mm = pe.matmul(GU[:, b, o1], at[:, b, lo_ + 2 * P:lo_ + 3 * P], vals[:, 1, :], start=False, stop=True)
                        mm.then_inc(pv_ready, 1)
                gu2, dd02, dd13 = ([GU[:, 0, :], GU[:, 1, :]], [DD[:, 0, :], DD[:, 2, :]], [DD[:, 1, :], DD[:, 3, :]])
                pe.wait_ge(pv_used, 16)
                wait_xt()
                for q, dst in enumerate((gu2, dd02, dd13, gu2)):
                    if q == 3:
                        pe.wait_ge(br_used, 2)
                        fill(merged, 0)
                        fill(merged, 1)
                    x_half(dst, ent[n.next], 0, 4 * (q % 2), True, done=br_ready)
                    n.next += 1
                    if q == 0:
                        pe.wait_ge(yb_ready, 2)
                        for b in range(2):
                            fill(yb, b)
                        wait_xt()
                pending.update({0: [], 2: [], 4: [(merged, 2, 4), (merged, 3, 4)]})
                full_to_dd()

            pe.wait_ge(small_loaded, SMALL_LOADS * 16)
            pe.wait_ge(const_ready, 1)
            pe.transpose(TB[:, 0, 0:P], rows1[:, :], ident[:, :])
            pe.transpose(TB[:, 0, P:P + N_SM2], rows2[:, :], ident[0:N_SM2, 0:N_SM2]).then_inc(cols_t, 1)
            prep_x()
            ffn("ffn0")
            prep_x()
            for g in range(6):
                group("gu" if g % 2 == 0 else "d")
            pe_conv()
            full_to_dd()
            prep_x()
            ffn("ffn1")
            prep_x()
            for g in range(4):
                group("gu" if g % 2 == 0 else "d")
            wait_results()
            prep(ktok)
            prep(x, defer=True)
            ffn("ffn2")
            prep_x()
            for g in range(2):
                group("gu" if g % 2 == 0 else "d")
            wait_results()
            prep(ktok)
            wait_xt()
            pe_attention()
            pe.wait_ge(o_ready, 1)
            fill(otok, 0)
            fill(otok, 1)
            pending.update({0: [], 2: [], 4: [(otok, 2, 2), (otok, 3, 2)]})
            full_to_dd()
            prep_x()
            ffn("ffn3")
            prep_x()
            pe_mixers()
            prep_x()
            ffn("ff")
            assert n.next == len(ent)


        @block.scalar
        def _(act):
            n = Places()
            n.ssq = 0

            def split(e, d=0):
                if e.split:
                    s, size = e.slot, e.kt * e.cols
                    act.wait_ge(loaded[s], (d + e.raw_before + 1) * 32)
                    if e.split_before or not isinstance(d, int):
                        act.wait_ge(used[s], d + e.split_before)
                    nc.scalar.activation(whi[s][:, 0:size], raw[s][:, 0:size], ACT.Copy).then_inc(hi_done[s], 1)

            def split_to(i):
                while n.next < min(i, len(ent)):
                    split(ent[n.next])
                    n.next += 1

            def prep(cols, kts=KT):
                for b in range(kts // 2):
                    bank = b % 2
                    n.t[bank] += 1
                    act.wait_ge(t_ready[bank], n.t[bank])
                    for j in range(2):
                        ins = nc.scalar.activation(xh[:, 2 * b + j, :], TB[:, bank, j * S:(j + 1) * S], ACT.Copy,
                                                   scale=cols(2 * b + j))
                    ins.then_inc(xh_done, 1)

            def sumsq(name, src):
                for t in range(TT):
                    c = ncol[name] + t
                    if n.ssq:
                        act.wait_ge(ssq_ready, n.ssq)
                    n.ssq += 1
                    nc.scalar.activation(junk[:, :], src(t), ACT.Square, accum_out=ssq[:, c:c + 1]).then_inc(ssq_ready, 1)

            def prep_x(name, then, fresh=True):
                n.x += fresh
                if n.x == 1:
                    act.wait_ge(x_loaded, 16)
                    act.wait_ge(cols_ready, 2)
                split_to(seg[then] + (1 if then == "ffn0" else 2))
                prep(PRE[name])
                if fresh:
                    if n.x > 1:
                        act.wait_ge(x_ready, 4 * (n.x - 1))
                    sumsq(name, lambda t: x[:, t, :])
                split_to(seg[then] + st.allow[then])

            def evacuate(name, seg_name, groups, dst, scale=None):
                base = seg[seg_name]
                for g in range(groups):
                    if g % 2 == 0:
                        n.gu += 1
                        act.wait_ge(gu_ready, n.gu)
                        src, read = GU[:, 0, :], gu_used[0]
                    else:
                        n.d += 1
                        act.wait_ge(d_ready, n.d)
                        src, read = DD[:, 0, :], d_used[0]
                    if g == 0:
                        act.wait_ge(rs_ready, ncol[name] + 2)
                        if scale is not None:
                            act.wait_ge(r8_ready, 1)
                    m = ent[base + 2 * g].cols
                    nc.scalar.activation(dst(g, 0), src[:, 0:m], ACT.Copy,
                                         scale=rcol(name, 0) if scale is None else scale[:, 0:1]).then_inc(read, 1)
                    if g + 2 < groups:
                        split_to(base + 2 * (g + 2) + 2)

            def ffn(name, pre):
                steps, nd = ffn_shape(name)
                per, t0, gu0 = 2 + nd, list(n.t), n.gu
                base = seg[name]
                slot1 = ent[base + 1].split_before

                def hidden_hi(g, d):
                    for b in range(nd):
                        act.wait_ge(t_ready[b], d + t0[b] + g + 1)
                        nc.scalar.activation(hth[:, 2 * b:2 * b + 2, :].rearrange("p k n -> p (k n)"), TB[:, b, :],
                                             ACT.Copy).then_inc(hth_done[b], 1)

                def gate(g, d):
                    for t in range(TT):
                        if t == 0:
                            act.wait_ge(gu_ready, d + gu0 + g + 1)
                        else:
                            act.wait_ge(used[1], d + slot1 + g + 1)
                        if nd == 1:
                            nc.scalar.activation(sg[:, t, 0:FG], GU[:, t, 0:FG], ACT.Silu,
                                                 scale=rcol(pre, t)).then_inc(sg_done[t], 1)
                        else:
                            nc.scalar.activation(sg[:, t, :], GU[:, t, :], ACT.Relu,
                                                 scale=rcol(pre, t)).then_inc(gu_used[t], 1)

                def step(g, e, d=0):
                    for q in range(nd):
                        split(ent[e + q], d)
                    hidden_hi(g - 1, d)
                    split(ent[e + nd], d)
                    gate(g, d)
                    split(ent[e + nd + 1], d)

                split_to(base + 2)
                act.wait_ge(rs_ready, ncol[pre] + 2)
                split(ent[base + 2])
                gate(0, 0)
                split(ent[base + 3])
                step(1, base + 4)
                with act.Fori(0, steps - 3) as i:
                    step(2, base + 4 + per, i)
                e = base + 4 + per * (steps - 2)
                for q in range(nd):
                    split(ent[e + q])
                hidden_hi(steps - 2, 0)
                gate(steps - 1, 0)
                for q in range(nd):
                    split(ent[e + nd + q])
                hidden_hi(steps - 1, 0)
                n.next = e + 2 * nd
                n.gu = gu0 + steps
                for b in range(nd):
                    n.t[b] = t0[b] + steps

            def post(i, then):
                last = ent[seg[then] - 1]
                split_to(seg[then] + 2)
                n.d += 1
                for t in range(TT):
                    if t == 0:
                        act.wait_ge(d_ready, n.d)
                    else:
                        act.wait_ge(used[last.slot], last.split_before + 1)
                    c = ncol[f"post{i}"] + t
                    act.wait_ge(ssq_ready, n.ssq)
                    n.ssq += 1
                    nc.scalar.activation(junk[:, :], DD[:, 2 * t:2 * t + 2, :].rearrange("p a n -> p (a n)"),
                                         ACT.Square, accum_out=ssq[:, c:c + 1]).then_inc(ssq_ready, 1)

            def act_conv():
                for k in range(KT + 1):
                    if k < KT:
                        n.t[k % 2] += 1
                        act.wait_ge(t_ready[k % 2], n.t[k % 2])
                        nc.scalar.activation(cpad[:, k % 2, 2:2 + S], TB[:, k % 2, 0:S], ACT.Copy).then_inc(cu_copied, 1)
                    if k:
                        j = k - 1
                        act.wait_ge(t_used[j % 2], n.t[j % 2])
                        nc.scalar.activation(xh[:, j, :], zb[:, j % 2, :], ACT.Copy).then_inc(xh_done, 1)

            def act_copy_transposed(dst):
                for b in range(4):
                    n.t[b % 2] += 1
                    if b % 2 == 0:
                        act.wait_ge(t_ready[0], n.t[0])
                        nc.scalar.activation(dst[:, 2 * b:2 * b + 2, :].rearrange("p k n -> p (k n)"), TB[:, 0, :],
                                             ACT.Copy).then_inc(t_used[0], 1)

            def act_attention():
                split_to(seg["o"] + 2)
                act.wait_ge(lam_sums, 1)
                nc.scalar.activation(lexp, lsum, ACT.Exp).then_inc(lam_exp, 1)
                for u in range(10):
                    if u < 8:
                        act.wait_ge(mx_ready, u + 1)
                        b = u % 2
                        for c in range(2):
                            for qi in range(TT):
                                e = nc.scalar.activation(sm[:, b, c, keys(qi)], sm[:, b, c, keys(qi)], ACT.Exp,
                                                         bias=nmx[:, b, c, qi:qi + 1], accum_out=den[:, b, c, qi:qi + 1])
                        e.then_inc(exp_done, 1)
                    if 1 <= u < 9:
                        b = (u - 1) % 2
                        n.t[b] += 1
                        act.wait_ge(t_ready[b], n.t[b])
                        if u >= 3:
                            act.wait_ge(pv_ready, u - 2)
                        nc.scalar.activation(at[:, b, 0:3 * P], TB[:, b, 0:3 * P], ACT.Copy).then_inc(t_used[b], 1)
                    if u >= 2:
                        h, b = u - 2, u % 2
                        act.wait_ge(pv_ready, h + 1)
                        nc.scalar.activation(otok[:, :, h * P:(h + 1) * P],
                                             GU[:, b, 0:2 * P].rearrange("p (t e) -> p t e", t=TT), ACT.Copy)\
                            .then_inc(pv_used, 1)


            def act_mixers():
                def group(g):
                    if g in (1, 3):
                        n.d += 1
                        act.wait_ge(d_ready, n.d)
                        src, read = DD[:, 0, :], d_used[0]
                    else:
                        n.gu += 1
                        act.wait_ge(gu_ready, n.gu)
                        src, read = GU[:, 0, :], gu_used[0]
                    if g == 0:
                        act.wait_ge(rs_ready, ncol["pre7"] + 2)
                    m = ent[seg["w_in"] + 2 * g].cols
                    nc.scalar.activation(P3(512 * g, m)[:, 0, :], src[:, 0:m], ACT.Copy, scale=rcol("pre7", 0)).then_inc(read, 1)
                    if g < 9:
                        split_to(seg["w_in"] + 2 * (g + 2) + 2)

                act.wait_ge(lbt_ready, 1)
                nc.scalar.activation(lbe, lbt, ACT.Exp).then_inc(lbe_ready, 1)
                for g in range(3):
                    group(g)

                def bank(b):
                    n.t[b] += 1
                    act.wait_ge(t_ready[b], n.t[b])

                for b in range(2):
                    bank(b)
                    nc.scalar.activation(hq[:, b * 512:(b + 1) * 512], TB[:, b, :], ACT.Copy).then_inc(t_used[b], 1)
                for b in range(2):
                    bank(b)
                    nc.scalar.activation(hf[:, b * 512:(b + 1) * 512], TB[:, b, :], ACT.Sigmoid).then_inc(t_used[b], 1)
                act.wait_ge(f_ready, 1)
                nc.scalar.activation(hx, hf, ACT.Ln).then_inc(lf_ready, 1)
                group(3)
                act.wait_ge(b_ready, 1)
                nc.scalar.activation(he, hf, ACT.Exp).then_inc(e_ready, 1)
                nc.scalar.activation(hx, hf, ACT.Exp, scale=-1.0).then_inc(e_ready, 1)
                act.wait_ge(bd_ready, 1)
                nc.scalar.activation(hf, hf, ACT.Exp).then_inc(el_ready, 1)
                group(4)
                act.wait_ge(d_used[0], n.d)
                act.wait_ge(d_used[1], n.d)
                nc.scalar.activation(P3(C_G, 512), P3(C_G, 512), ACT.Silu).then_inc(gates_ready, 1)
                group(5)
                for b in range(2):
                    bank(b)
                    nc.scalar.activation(kltok[:, b * 512:(b + 1) * 512], TB[:, b, :], ACT.Copy).then_inc(t_used[b], 1)
                group(6)
                act.wait_ge(red_ready, 1)
                nc.scalar.activation(trig, red, ACT.Sin).then_inc(trig_ready, 1)
                group(7)
                act.wait_ge(ho_ready, 1)
                nc.scalar.activation(ya[:, 0, :], DD[:, 3, :], ACT.Copy).then_inc(ho_copied, 1)
                group(8)
                bank(0)
                nc.scalar.activation(P3(C_F, 512)[:, 0, :], TB[:, 0, :], ACT.Copy, scale=0.125).then_inc(t_used[0], 1)
                bank(0)
                tb = TB[:, 0, :].rearrange("p (g n) -> p g n", g=2)
                nc.scalar.activation(kc2[0:64, :, :], tb[0:64], ACT.Copy)
                nc.scalar.activation(kc2[64:P, :, 0:S - 1], tb[64:P, :, 1:S], ACT.Copy).then_inc(t_used[0], 1)
                bank(0)
                nc.scalar.activation(g1_[:, 0:512], TB[:, 0, :], ACT.Copy).then_inc(t_used[0], 1)
                n.t[1] += 3
                group(9)
                es = ent[seg["cmp"]:seg["cmp"] + 4]
                for i in range(2):
                    e = es[2 * i + 1]
                    act.wait_ge(lo_done[e.slot], e.raw_before + 1)
                    nc.scalar.activation(gel[:, i, :], DD[0:2 * NCMP, i, 0:S], ACT.Gelu_apprx_tanh).then_inc(gelu_ready, 1)
                group(10)
                act.wait_ge(gu_used[0], n.gu)
                act.wait_ge(gu_used[1], n.gu)
                nc.scalar.activation(gate_cols, gate_cols, ACT.Sigmoid).then_inc(gates_ready, 1)
                bank(0)
                n.t[1] += 1
                nc.scalar.activation(g1k, TB[:, 0, 0:64].rearrange("p (h n) -> p h n", h=2)[:, :, 0:30], ACT.Copy)\
                    .then_inc(t_used[0], 1)
                act.wait_ge(cmp_ready, 1)
                nc.scalar.activation(kcT, DD[:, 2, 0:30], ACT.Copy).then_inc(kcT_ready, 1)
                prep_at(lambda k: col2[:, R_HG:R_HG + 1], 0)
                split_to(seg["branch"] + 2)
                act.wait_ge(cmx_ready, 1)
                nc.scalar.activation(csc, csc, ACT.Exp).then_inc(cexp_ready, 1)
                bank(0)
                nc.scalar.activation(pcT, TB[0:120, 0, 0:S], ACT.Copy).then_inc(t_used[0], 1)
                nc.scalar.activation(P3(C_MG, 2 * D), P3(C_MG, 2 * D), ACT.Sigmoid).then_inc(gates_ready, 1)
                for u in range(UNITS + 1):
                    if u < UNITS:
                        act.wait_ge(mx_ready, 8 + u + 1)
                        b = u % 2
                        for c in range(2):
                            for qi in range(TT):
                                e = nc.scalar.activation(sm[:, b, c, keys(qi)], sm[:, b, c, keys(qi)], ACT.Exp,
                                                         bias=nmx[:, b, c, qi:qi + 1], accum_out=den[:, b, c, qi:qi + 1])
                        e.then_inc(exp_done, 1)
                    if u >= 1:
                        v, b = u - 1, (u - 1) % 2
                        act.wait_ge(pv_ready, 8 + max(v - 1, 0))
                        for i in range(2):
                            bank(i)
                            nc.scalar.activation(at[:, b, 3 * P * i:3 * P * (i + 1)], TB[:, i, 0:3 * P], ACT.Copy)\
                                .then_inc(t_used[i], 1)
                split_to(seg["branch"] + 4)
                prep_at(lambda k: 1.0, 4)
                split_to(seg["w_out"] + 2)
                prep_at(lambda k: 1.0, 0, KT)
                split_to(seg["w_out"] + 4)
                split_to(seg["ff"] + 2)
                n.d += 1

            def prep_at(cols, k0, kts=4):
                for b in range(kts // 2):
                    n.t[b % 2] += 1
                    act.wait_ge(t_ready[b % 2], n.t[b % 2])
                    for j in range(2):
                        ins = nc.scalar.activation(xh[:, k0 + 2 * b + j, :], TB[:, b % 2, j * S:(j + 1) * S], ACT.Copy,
                                                   scale=cols(j))
                    ins.then_inc(xh_done, 1)

            act.dma_start(rows1[0:96, :], a["g_norm"].rearrange("l j (k p) -> (l j k) p", p=P)).then_inc(small_loaded, 16)
            for row, src in ((R_GKV, a["g_kv"]), (R_N1, a["norm1_g_2"][0]), (R_N2, a["norm2_g_2"][0])):
                act.dma_start(rows1[row:row + 8, :], src.rearrange("(k p) -> k p", p=P)).then_inc(small_loaded, 16)
            act.dma_start(rows1[R_LB:P, :], a["lb_param_2"].rearrange("l (k p) -> (l k) p", p=P)).then_inc(small_loaded, 16)
            act.dma_start(rows2[0:R_PEK, :], a["w_conv"][0].rearrange("j (k p) -> (j k) p", p=P)).then_inc(small_loaded, 16)
            for row, src in ((R_PEK, a["cmp_pe_k_2"][0]), (R_PEV, a["cmp_pe_v_2"][0])):
                act.dma_start(rows2[row:row + 16, :], src.rearrange("(k j) d -> k (j d)", j=2)).then_inc(small_loaded, 16)
            act.dma_start(rows2[R_SUB:R_SUB + 1, :], a["g_subln"]).then_inc(small_loaded, 16)
            act.dma_start(rows2[R_HG:R_HG + 1, :], a["hgrn_norm_g_2"]).then_inc(small_loaded, 16)
            act.wait_ge(cols_t, 1)
            nc.scalar.activation(col1[:, :], TB[:, 0, 0:P], ACT.Copy).then_inc(cols_ready, 1)
            nc.scalar.activation(col2[:, :], TB[:, 0, P:P + N_SM2], ACT.Copy).then_inc(cols_ready, 1)
            prep_x("pre0", "ffn0")
            ffn("ffn0", "pre0")
            post(0, "conv_in")
            prep_x("pre1", "conv_in")
            evacuate("pre1", "conv_in", 6, lambda g, t: P3(512 * g, 512, 0, 3072)[:, t, :])
            act_conv()
            split_to(seg["conv_out"] + 4)
            post(1, "ffn1")
            prep_x("pre2", "ffn1")
            ffn("ffn1", "pre2")
            post(2, "kv")
            prep_x("pre3", "kv")
            evacuate("pre3", "kv", 4, kv_dst)
            act_copy_transposed(kT)
            prep_x("pre4", "ffn2", fresh=False)
            ffn("ffn2", "pre4")
            post(3, "q")
            prep_x("pre5", "q")
            evacuate("pre5", "q", 2, kv_dst, scale=r8)
            act_copy_transposed(qT)
            act_attention()
            act.wait_ge(gsub_ready, 1)
            for k0 in (0, 4):
                prep_at(lambda k: gsub[:, 0:1], k0)
            split_to(seg["o"] + 4)
            post(4, "ffn3")
            prep_x("pre6", "ffn3")
            ffn("ffn3", "pre6")
            post(5, "w_in")
            prep_x("pre7", "w_in")
            act_mixers()
            prep_x("pre8", "ff")
            ffn("ff", "pre8")
            act.wait_ge(x_ready, 4 * n.x)
            sumsq("final", lambda t: x[:, t, :])

        @block.vector
        def _(dve):
            n = Places()
            n.sg, n.chain = 0, 0

            def chain(ins):
                n.chain += 1
                ins.then_inc(dve_chain, 1)
                dve.wait_ge(dve_chain, n.chain)

            def split(e, d=0):
                if e.split:
                    s, size = e.slot, e.kt * e.cols
                    dve.wait_ge(hi_done[s], d + e.split_before + 1)
                    nc.vector.tensor_tensor(wlo[s][:, 0:size], raw[s][:, 0:size], whi[s][:, 0:size].bitcast(F32),
                                            ALU.subtract).then_inc(lo_done[s], 1)

            def split_to(i):
                while n.next < min(i, len(ent)):
                    split(ent[n.next])
                    n.next += 1

            def prep(cols, kts=KT):
                for b in range(kts // 2):
                    bank = b % 2
                    n.t[bank] += 1
                    n.xh += 1
                    dve.wait_ge(xh_done, n.xh)
                    for j in range(2):
                        k = 2 * b + j
                        ins = nc.vector.scalar_tensor_tensor(
                            out=xl[:, k, :], in0=TB[:, bank, j * S:(j + 1) * S], scalar=cols(k),
                            in1=xh[:, k, :].bitcast(F32), op0=ALU.mult, op1=ALU.subtract)
                    ins.then_inc(t_used[bank], 1)

            def prep_x(name, then):
                split_to(seg[then] + (1 if then == "ffn0" else 2))
                prep(PRE[name])
                split_to(seg[then] + st.allow[then])

            def evacuate(name, seg_name, groups, dst, scale=None, after=None):
                base = seg[seg_name]
                dve.wait_ge(rs_ready, ncol[name] + 2)
                if scale is not None:
                    dve.wait_ge(r8_ready, 1)
                for g in range(groups):
                    e = ent[base + 2 * g + 1]
                    dve.wait_ge(used[e.slot], e.split_before + 1)
                    if g % 2 == 0:
                        n.gu += 1
                        src, read = GU[:, 1, :], gu_used[1]
                    else:
                        n.d += 1
                        src, read = DD[:, 2, :], d_used[1]
                    nc.vector.tensor_scalar(dst(g, 1), src[:, 0:e.cols], rcol(name, 1) if scale is None else scale[:, 1:2],
                                            None, ALU.mult).then_inc(read, 1)
                    if after:
                        after(g)
                    if g + 2 < groups:
                        split_to(base + 2 * (g + 2) + 2)

            def wait_results():
                for t in range(TT):
                    dve.wait_ge(gu_used[t], n.gu)
                    dve.wait_ge(d_used[t], n.d)

            def ffn(name, pre):
                steps, nd = ffn_shape(name)
                per, gu0, sg0, hth0 = 2 + nd, n.gu, n.sg, n.hth
                base = seg[name]

                def hidden_lo(g, d):
                    for b in range(nd):
                        dve.wait_ge(hth_done[b], d + (hth0 if b == 0 else 0) + g + 1)
                        nc.vector.tensor_tensor(htl[:, 2 * b:2 * b + 2, :].rearrange("p k n -> p (k n)"), TB[:, b, :],
                                                hth[:, 2 * b:2 * b + 2, :].rearrange("p k n -> p (k n)").bitcast(F32),
                                                ALU.subtract).then_inc(t_used[b], 1)

                def hidden(g, d):
                    for t in range(TT):
                        if nd == 1:
                            dve.wait_ge(sg_done[t], d + sg0 + g + 1)
                            nc.vector.scalar_tensor_tensor(out=hid[:, t, 0:FG], in0=GU[:, t, FG:512], scalar=rcol(pre, t),
                                                           in1=sg[:, t, 0:FG], op0=ALU.mult, op1=ALU.mult)\
                                .then_inc(gu_used[t], 1)
                        else:
                            dve.wait_ge(gu_used[t], d + gu0 + g + 1)
                            nc.vector.tensor_tensor(hid[:, t, :], sg[:, t, :], sg[:, t, :], ALU.mult)\
                                .then_inc(h_ready[t], 1)

                def step(g, e, d=0):
                    for q in range(nd):
                        split(ent[e + q], d)
                    hidden_lo(g - 1, d)
                    split(ent[e + nd], d)
                    hidden(g, d)
                    split(ent[e + nd + 1], d)

                split_to(base + 2)
                dve.wait_ge(rs_ready, ncol[pre] + 2)
                split(ent[base + 2])
                hidden(0, 0)
                split(ent[base + 3])
                step(1, base + 4)
                with dve.Fori(0, steps - 3) as i:
                    step(2, base + 4 + per, i)
                e = base + 4 + per * (steps - 2)
                for q in range(nd):
                    split(ent[e + q])
                hidden_lo(steps - 2, 0)
                hidden(steps - 1, 0)
                for q in range(nd):
                    split(ent[e + nd + q])
                hidden_lo(steps - 1, 0)
                n.next = e + 2 * nd
                n.gu = gu0 + steps
                n.hth += steps
                for b in range(nd):
                    n.t[b] += steps
                if nd == 1:
                    n.sg += steps

            def post(i, then):
                split_to(seg[then] + 2)
                n.d += 1
                dve.wait_ge(gain_loaded[i % 2], 16 * (i // 2 + 1))
                for t in range(TT):
                    dve.wait_ge(ssq_ready, ncol[f"post{i}"] + t + 1)
                    halves = [slice(512 * nn, 512 * nn + 512) for nn in range(2)]
                    for nn, cs in enumerate(halves):
                        ins = nc.vector.scalar_tensor_tensor(out=tmp[:, t, cs], in0=DD[:, 2 * t + nn, :], scalar=HALF[i],
                                                             in1=gain[:, i % 2, cs], op0=ALU.mult, op1=ALU.mult)
                    ins.then_inc(d_used[t], 1)
                    dve.wait_ge(rs_ready, ncol[f"post{i}"] + t + 1)
                    dve.wait_ge(d_used[t], n.d)
                    for cs in halves:
                        nc.vector.scalar_tensor_tensor(out=x[:, t, cs], in0=tmp[:, t, cs], scalar=rcol(f"post{i}", t),
                                                       in1=x[:, t, cs], op0=ALU.mult, op1=ALU.add).then_inc(x_ready, 1)
                n.x += 1

            def dve_setup():
                dve.wait_ge(cols_ready, 2)
                nc.vector.tensor_scalar(gsub, col2[:, R_SUB:R_SUB + 1], 1.0 - LAMBDA_INIT, None, ALU.mult).then_inc(gsub_ready, 1)

            def dve_cu(g):
                if g >= 4:
                    i = g - 4
                    p3 = P3(0, 3 * D, 0, 3 * D)
                    for t in range(TT):
                        if i == 0:
                            dve.wait_ge(gu_used[t], n.gu)
                        else:
                            dve.wait_ge(d_used[t], n.d)
                    cs = slice(D + 512 * i, D + 512 * i + 512)
                    us = slice(2 * D + 512 * i, 2 * D + 512 * i + 512)
                    nc.vector.tensor_tensor(p3[:, :, cs], p3[:, :, cs], p3[:, :, us], ALU.mult).then_inc(cu_ready, 1)

            def dve_conv():
                def lo(k):
                    n.xh += 1
                    dve.wait_ge(xh_done, n.xh)
                    nc.vector.tensor_tensor(xl[:, k, :], zb[:, k % 2, :], xh[:, k, :].bitcast(F32), ALU.subtract)\
                        .then_inc(conv_split, 1)

                chain(nc.vector.memset(cpad[:, :, 0:2], 0.0))
                for k in range(KT):
                    b = k % 2
                    zacc = zaccs[b]
                    n.t[b] += 1

                    def w(j):
                        return col2[:, 8 * j + k:8 * j + k + 1]

                    dve.wait_ge(cu_copied, k + 1)
                    chain(nc.vector.tensor_scalar(zacc, cpad[:, b, 2:2 + S], w(2), None, ALU.mult))
                    chain(nc.vector.scalar_tensor_tensor(out=zacc, in0=cpad[:, b, 1:1 + S], scalar=w(1), in1=zacc,
                                                         op0=ALU.mult, op1=ALU.add))
                    chain(nc.vector.scalar_tensor_tensor(out=zacc, in0=cpad[:, b, 0:S], scalar=w(0), in1=zacc,
                                                         op0=ALU.mult, op1=ALU.add))
                    nc.vector.tensor_tensor(zb[:, b, :], zacc, TB[:, b, S:2 * S], ALU.mult).then_inc(t_used[b], 1)
                    if k:
                        lo(k - 1)
                lo(KT - 1)

            def dve_copy_transposed(dst):
                for b in range(4):
                    n.t[b % 2] += 1
                    if b % 2:
                        dve.wait_ge(t_ready[1], n.t[1])
                        nc.vector.tensor_copy(dst[:, 2 * b:2 * b + 2, :].rearrange("p k n -> p (k n)"), TB[:, 1, :])\
                            .then_inc(t_used[1], 1)

            def masked_scores(u, bias_):
                b = u % 2
                dve.wait_ge(sc_ready, u + 1)
                nc.vector.tensor_tensor(sm[:, b, :, :], DD[:, 2 * b:2 * b + 2, 0:3 * P],
                                        mask3[:, :].unsqueeze(1).broadcast_to([P, 2, 3 * P]), ALU.add).then_inc(sc_used, 1)
                dve.wait_ge(sc_used, u + 1)
                nc.vector.tensor_reduce(nmx[:, b, :, 0], sm[:, b, :, keys(0)], AX.X, ALU.max)
                chain(nc.vector.tensor_reduce(nmx[:, b, :, 1], sm[:, b, :, keys(1)], AX.X, ALU.max))
                nc.vector.tensor_scalar(nmx[:, b, :, :], nmx[:, b, :, :], -1.0, None, ALU.mult).then_inc(mx_ready, 1)

            def dve_attention():
                split_to(seg["o"] + 2)
                dve.wait_ge(lam_loaded, 64)
                lp = lamv[:, 0:3:2, :]
                chain(nc.vector.tensor_tensor(lp, lp, lamv[:, 1:4:2, :], ALU.mult))
                nc.vector.tensor_reduce(lsum, lp, AX.X, ALU.add).then_inc(lam_sums, 1)
                dve.wait_ge(lam_exp, 1)
                chain(nc.vector.scalar_tensor_tensor(out=nlam, in0=lexp[:, 1:2], scalar=-LAMBDA_INIT, in1=lexp[:, 0:1],
                                                     op0=ALU.add, op1=ALU.subtract))
                t0 = list(n.t)
                for u in range(9):
                    if 2 <= u < 8:
                        dve.wait_ge(a_ready, u - 1)
                    if u < 8:
                        masked_scores(u, 0)
                    if u >= 1:
                        v, b = u - 1, (u - 1) % 2
                        dve.wait_ge(exp_done, u)
                        chain(nc.vector.reciprocal(rden[:, b, :, :], den[:, b, :, :]))
                        chain(nc.vector.tensor_scalar(rl[:, b, :], rden[:, b, 1, :], nlam, None, ALU.mult))
                        for qi in range(TT):
                            ins = nc.vector.tensor_scalar(sm[:, b, 1, keys(qi)], sm[:, b, 1, keys(qi)], rl[:, b, qi:qi + 1],
                                                          None, ALU.mult)
                        chain(ins)
                        if v >= 2:
                            dve.wait_ge(t_ready[b], t0[b] + v // 2)
                        for qi in range(TT):
                            ins = nc.vector.scalar_tensor_tensor(
                                out=psc[:, b, keys(qi)], in0=sm[:, b, 0, keys(qi)], scalar=rden[:, b, 0, qi:qi + 1],
                                in1=sm[:, b, 1, keys(qi)], op0=ALU.mult, op1=ALU.add)
                        ins.then_inc(a_ready, 1)
                n.t = [t0[0] + 4, t0[1] + 4]
                head_norm(0)
                prep_at(lambda k: gsub[:, 0:1], 0)
                head_norm(1)
                prep_at(lambda k: gsub[:, 0:1], 4)

            def head_norm(i):
                dve.wait_ge(pv_used, 4 * i + 4)
                o_half = otok[:, :, 512 * i:512 * i + 512]
                sq = flat[:, 1024 * i:1024 * i + 1024]
                chain(nc.vector.tensor_tensor(sq.rearrange("p (t n) -> p t n", t=TT), o_half, o_half, ALU.mult))
                nc.vector.tensor_reduce(oss[:, 8 * i:8 * i + 8], sq.rearrange("p (a e) -> p a e", e=P), AX.X, ALU.add)\
                    .then_inc(oss_ready, 1)
                dve.wait_ge(ro_ready, i + 1)
                for t in range(TT):
                    ot = o_half[:, t, :].rearrange("p (h e) -> p h e", e=P)
                    ins = nc.vector.tensor_tensor(ot, ot, ro[:, 8 * i + 4 * t:8 * i + 4 * t + 4].unsqueeze(2)
                                                  .broadcast_to([P, 4, P]), ALU.mult)
                ins.then_inc(o_ready, 1)

            def dve_final():
                n.d += 1
                for t in range(TT):
                    if t == 0:
                        dve.wait_ge(d_ready, n.d)
                    else:
                        last = ent[-1]
                        dve.wait_ge(used[last.slot], last.split_before + 1)
                    for nn in range(2):
                        cs = slice(512 * nn, 512 * nn + 512)
                        nc.vector.tensor_tensor(x[:, t, cs], x[:, t, cs], DD[:, 2 * t + nn, :], ALU.add).then_inc(x_ready, 1)
                dve.wait_ge(gain_loaded[0], 64)
                for t in range(TT):
                    dve.wait_ge(rs_ready, ncol["final"] + t + 1)
                    nc.vector.scalar_tensor_tensor(out=tmp[:, t, :], in0=x[:, t, :], scalar=rcol("final", t),
                                                   in1=gain[:, 0, :], op0=ALU.mult, op1=ALU.mult).then_inc(out_ready, 1)


            def dve_mixers():
                l0, l1 = col1[:, R_LB:R_LB + 4], col1[:, R_LB + 4:R_LB + 8]
                chain(nc.vector.tensor_tensor(lbs, l0, l1, ALU.max))
                nc.vector.tensor_tensor(lbt[:, 0:4], l0, lbs, ALU.subtract)
                nc.vector.tensor_tensor(lbt[:, 4:8], l1, lbs, ALU.subtract).then_inc(lbt_ready, 1)
                dve.wait_ge(lbe_ready, 1)
                chain(nc.vector.tensor_tensor(lbs, lbe[:, 0:4], lbe[:, 4:8], ALU.add))
                chain(nc.vector.reciprocal(lbs, lbs))
                chain(nc.vector.tensor_tensor(lb, lbe[:, 0:4], lbs, ALU.mult))
                chain(nc.vector.tensor_scalar(omlb, lb, -1.0, 1.0, ALU.mult, ALU.add))

                def group(g):
                    e = ent[seg["w_in"] + 2 * g + 1]
                    dve.wait_ge(used[e.slot], e.split_before + 1)
                    if g in (1, 3):
                        n.d += 1
                        src, read = DD[:, 2, :], d_used[1]
                    else:
                        n.gu += 1
                        src, read = GU[:, 1, :], gu_used[1]
                    nc.vector.tensor_scalar(P3(512 * g, e.cols)[:, 1, :], src[:, 0:e.cols], rcol("pre7", 1),
                                            None, ALU.mult).then_inc(read, 1)
                    if g < 9:
                        split_to(seg["w_in"] + 2 * (g + 2) + 2)

                dve.wait_ge(rs_ready, ncol["pre7"] + 2)
                for g in range(3):
                    group(g)
                for b in range(2):
                    n.t[b] += 2
                    dve.wait_ge(t_used[b], n.t[b])
                for h in range(HGRN_H):
                    ins = nc.vector.tensor_scalar(heads4(hf)[:, h, :], heads4(hf)[:, h, :], omlb[:, h:h + 1], lb[:, h:h + 1],
                                                  ALU.mult, ALU.add)
                ins.then_inc(f_ready, 1)
                dve.wait_ge(f_ready, 1)
                chain(nc.vector.tensor_scalar(hk, hf, -1.0, 1.0, ALU.mult, ALU.add))
                dve.wait_ge(lf_ready, 1)
                dve.wait_ge(const2, 1)
                for h in range(HGRN_H):
                    ins = nc.vector.tensor_tensor_scan(heads4(hf)[:, h, :], coef, heads4(hx)[:, h, :], 0.0, ALU.mult, ALU.add)
                ins.then_inc(b_ready, 1)
                dve.wait_ge(b_ready, 1)
                chain(nc.vector.tensor_copy(bl, hf[:, CH - 1::CH]))
                group(3)
                dve.wait_ge(e_ready, 1)
                nc.vector.tensor_tensor(hq, hq, he, ALU.mult).then_inc(kd_ready, 1)
                dve.wait_ge(e_ready, 2)
                nc.vector.tensor_tensor(hx, hx, hk, ALU.mult).then_inc(kd_ready, 1)
                b16 = hf.rearrange("p (a n) -> p a n", n=CH)
                nc.vector.tensor_tensor(b16, bl.unsqueeze(2).broadcast_to([P, 16, CH]), b16, ALU.subtract).then_inc(bd_ready, 1)
                chain(nc.vector.memset(amask, 0.0))
                group(4)
                for t in range(TT):
                    dve.wait_ge(attn_ready, t + 1)
                    nc.vector.copy_predicated(amask[:, t, :].rearrange("p (h n) -> p h n", h=4),
                                              m64.bitcast(I32).unsqueeze(1).broadcast_to([P, 4, P]),
                                              DD[:, t, :].rearrange("p (h n) -> p h n", h=4)).then_inc(am_ready, 1)
                dve.wait_ge(el_ready, 1)
                dve.wait_ge(kd_ready, 2)
                nc.vector.tensor_tensor(hk, hk, hf, ALU.mult).then_inc(kl_ready, 1)
                trig_angles()
                group(5)
                for b in range(2):
                    n.t[b] += 1
                group(6)
                banks = [DD[:, 2, :], DD[:, 3, :], DD[:, 0, :]]
                for i in range(3):
                    dve.wait_ge(kv_ready, i + 1)
                    if i == 0:
                        nc.vector.tensor_copy(states[:, 0, :], banks[0]).then_inc(st_ready, 1)
                    else:
                        dve.wait_ge(st_ready, i)
                        for h in range(HGRN_H):
                            hs = slice(h * P, (h + 1) * P)
                            end = h * S + CH * i + CH - 1
                            ins = nc.vector.scalar_tensor_tensor(out=states[:, i, hs], in0=states[:, i - 1, hs],
                                                                 scalar=he[:, end:end + 1], in1=banks[i][:, hs],
                                                                 op0=ALU.mult, op1=ALU.add)
                        ins.then_inc(st_ready, 1)
                for t in range(TT):
                    dve.wait_ge(gu_used[t], n.gu)
                rope()
                group(7)
                dve.wait_ge(ho_ready, 2)
                nc.vector.tensor_copy(ya[:, 1, :], DD[:, 2, :]).then_inc(ho_copied, 1)
                dve.wait_ge(ho_copied, 2)
                chain(nc.vector.tensor_tensor(hf.rearrange("p (t n) -> p t n", t=TT), ya, ya, ALU.mult))
                nc.vector.tensor_reduce(hss, hf.rearrange("p (a e) -> p a e", e=P), AX.X, ALU.add).then_inc(hss_ready, 1)
                dve.wait_ge(hr_ready, 1)
                for t in range(TT):
                    v_ = ya[:, t, :].rearrange("p (h e) -> p h e", e=P)
                    ins = nc.vector.tensor_tensor(v_, v_, hr[:, 4 * t:4 * t + 4].unsqueeze(2).broadcast_to([P, 4, P]), ALU.mult)
                chain(ins)
                dve.wait_ge(gates_ready, 1)
                nc.vector.tensor_tensor(ya, ya, P3(C_G, 512), ALU.mult).then_inc(ya_ready, 1)
                group(8)
                n.t[0] += 3

                def bank(b):
                    n.t[b] += 1
                    dve.wait_ge(t_ready[b], n.t[b])

                bank(1)
                nc.vector.tensor_scalar(P3(C_F, 512)[:, 1, :], TB[:, 1, :], 0.125, None, ALU.mult).then_inc(t_used[1], 1)
                bank(1)
                tb = TB[:, 1, :].rearrange("p (g n) -> p g n", g=2)
                nc.vector.tensor_copy(vc2[0:64, :, :], tb[0:64])
                nc.vector.tensor_copy(vc2[64:P, :, 0:S - 1], tb[64:P, :, 1:S]).then_inc(t_used[1], 1)
                bank(1)
                nc.vector.tensor_copy(g1_[:, 512:1024], TB[:, 1, :]).then_inc(t_used[1], 1)
                for i, (c2, f_, r0) in enumerate(((kc2, ff_k, R_PEK), (vc2, ff_v, R_PEV))):
                    if i == 0:
                        dve.wait_ge(t_used[0], n.t[0] - 1)
                    else:
                        dve.wait_ge(t_used[1], n.t[1] - 1)
                    by = c2.rearrange("p g (c s) -> p s g c", s=16)
                    for half in range(2):
                        ins = nc.vector.tensor_tensor(
                            f_[:, 8 * half:8 * half + 8, :, :], by[:, 0:16:2, :, half:half + 15],
                            col2[:, r0 + 8 * half:r0 + 8 * half + 8].unsqueeze(2).unsqueeze(3).broadcast_to([P, 8, 2, 15]), ALU.add)
                    ins.then_inc(ffk_ready, 1)
                for hh in range(2):
                    nc.vector.tensor_copy(w2kk[:, hh, :, :], w2k[:, hh, :].unsqueeze(1).broadcast_to([P, 2, 64]))
                group(9)
                group(10)
                n.t[0] += 1
                bank(1)
                for hh in range(2):
                    ins = nc.vector.tensor_copy(g1x[:, hh, :, :, :], TB[:, 1, 32 * hh:32 * hh + 30]
                                                .rearrange("p (g c) -> p g c", g=2).unsqueeze(2).broadcast_to([P, 2, 4, 15]))
                ins.then_inc(t_used[1], 1)
                dve.wait_ge(cmp_ready, 2)
                nc.vector.tensor_tensor(vbd.rearrange("p (h d) -> p h d", d=64), DD[0:120, 3, 0:64].unsqueeze(1).broadcast_to([120, 8, 64]),
                                        bdiag[0:120, :].unsqueeze(2).broadcast_to([120, 8, 64]), ALU.mult).then_inc(vbd_ready, 1)
                prep_at(lambda k: col2[:, R_HG:R_HG + 1], 0)
                dve.wait_ge(csc_ready, 1)

                def per(t_, i):
                    return t_[:, i * 120:(i + 1) * 120].rearrange("p (t j c) -> p t j c", t=TT, j=4)

                def mask_of(m_):
                    return m_.rearrange("p (t c) -> p t c", t=TT).unsqueeze(2).broadcast_to([P, TT, 4, 15])

                for i in range(2):
                    ins = nc.vector.tensor_tensor(per(csc, i), GU[:, i, 0:120].rearrange("p (t j c) -> p t j c", t=TT, j=4),
                                                  mask_of(cmask), ALU.mult)
                chain(ins)
                for i in range(2):
                    ins = nc.vector.tensor_tensor(per(csc, i), per(csc, i), mask_of(cneg), ALU.add)
                chain(ins)
                c16 = csc.rearrange("p (a c) -> p a c", c=15)
                chain(nc.vector.tensor_reduce(cmx, c16, AX.X, ALU.max))
                nc.vector.tensor_tensor(c16, c16, cmx.unsqueeze(2).broadcast_to([P, 16, 15]), ALU.subtract).then_inc(cmx_ready, 1)
                dve.wait_ge(cexp_ready, 1)
                for i in range(2):
                    ins = nc.vector.tensor_tensor(per(csc, i), per(csc, i), mask_of(cmask), ALU.mult)
                chain(ins)
                chain(nc.vector.tensor_reduce(cden, c16, AX.X, ALU.add))
                chain(nc.vector.tensor_scalar(cden, cden, 1e-30, None, ALU.max))
                chain(nc.vector.reciprocal(cden, cden))
                for i in range(2):
                    ins = nc.vector.tensor_tensor(pc.rearrange("p (t j i c) -> p t j i c", t=TT, j=4, i=2)[:, :, :, i, :], per(csc, i),
                                                  cden[:, 8 * i:8 * i + 8].rearrange("p (t j) -> p t j", t=TT).unsqueeze(3)
                                                  .broadcast_to([P, TT, 4, 15]), ALU.mult)
                ins.then_inc(pc_ready, 1)
                n.t[0] += 1
                split_to(seg["branch"] + 2)
                dve.wait_ge(gates_ready, 2)
                dve.wait_ge(oc_ready, 1)
                for t in range(TT):
                    ins = nc.vector.tensor_tensor(yb[:, t, :].rearrange("p (h d) -> p h d", d=64),
                                                  DD[:, t, :].rearrange("p (h d) -> p h d", d=64),
                                                  gate_cols[:, t, 0:24:3].unsqueeze(2).broadcast_to([P, 8, 64]), ALU.mult)
                ins.then_inc(yb_ready, 1)
                dve.wait_ge(yb_ready, 1)
                for u in range(UNITS + 2):
                    if u < UNITS:
                        if u >= 2:
                            for i in range(2):
                                dve.wait_ge(t_ready[i], n.t[i] + u - 1)
                        masked_scores(8 + u, 0)
                    if u >= 2:
                        v, b = u - 2, u % 2
                        br, j, g, _, _ = unit(v)
                        dve.wait_ge(pv_ready, 8 + v + 1)
                        gv = gate_cols[:, :, 3 * 2 * j + br + 1:3 * (2 * j + 2):3].rearrange("p t i -> p i t")
                        w_ = wgt[:, 4 * b:4 * b + 4].rearrange("p (i t) -> p i t", i=2)
                        chain(nc.vector.tensor_tensor(w_, rdens[v], gv, ALU.mult))
                        o4 = psc[:, b, 0:256].rearrange("p (a d) -> p a d", d=64)
                        nc.vector.tensor_tensor(o4, GU[:, b, 0:256].rearrange("p (a d) -> p a d", d=64),
                                                wgt[:, 4 * b:4 * b + 4].unsqueeze(2).broadcast_to([P, 4, 64]), ALU.mult)\
                            .then_inc(pv_used, 1)
                        dve.wait_ge(pv_used, 8 + v + 1)
                        yv = yb.rearrange("p t (h d) -> p h t d", d=64)[:, 2 * j:2 * j + 2, :, :]
                        chain(nc.vector.tensor_tensor(yv, yv, o4.rearrange("p (i t) d -> p i t d", i=2), ALU.add))
                    if 1 <= u < UNITS + 1:
                        v, b = u - 1, (u - 1) % 2
                        dve.wait_ge(exp_done, 8 + u)
                        chain(nc.vector.reciprocal(rden[:, b, :, :], den[:, b, :, :]))
                        rdens[v] = rden[:, b, :, :]
                nc.vector.memset(wgt[:, 0:1], 0.0).then_inc(yb_ready, 1)
                n.t[0] += UNITS
                n.t[1] += UNITS
                split_to(seg["branch"] + 4)
                prep_at(lambda k: 1.0, 4)
                dve.wait_ge(gates_ready, 3)
                for nn, (ya_at, yb_at) in enumerate((((GU, 0, 1), (DD, 0, 2)), ((DD, 1, 2), (GU, 0, 1)))):
                    eb = ent[seg["branch"] + 2 * nn + 1]
                    cs = slice(512 * nn, 512 * nn + 512)
                    for t in range(TT):
                        if t == 0:
                            dve.wait_ge(br_ready, 2 * nn + 2)
                        else:
                            dve.wait_ge(used[eb.slot], eb.split_before + 1)
                        pa, pb = (bank_[:, first + t * by_, :] for bank_, first, by_ in (ya_at, yb_at))
                        part = states[:, t, :]
                        nc.vector.tensor_tensor(merged[:, t, cs], pa, P3(C_MG + 512 * nn, 512)[:, t, :], ALU.mult)
                        chain(nc.vector.tensor_tensor(part, pb, P3(C_MG + D + 512 * nn, 512)[:, t, :], ALU.mult))
                        nc.vector.tensor_tensor(merged[:, t, cs], merged[:, t, cs], part, ALU.add).then_inc(br_used, 1)
                        dve.wait_ge(br_used, 2 * nn + t + 1)
                    if nn == 0:
                        prep_at(lambda k: 1.0, 0)
                        split_to(seg["w_out"] + 2)
                    else:
                        prep_at(lambda k: 1.0, 4)
                split_to(seg["w_out"] + 4)
                split_to(seg["ff"] + 2)
                n.d += 1
                last = ent[seg["ff"] - 1]
                for t in range(TT):
                    if t == 0:
                        dve.wait_ge(d_ready, n.d)
                    else:
                        dve.wait_ge(used[last.slot], last.split_before + 1)
                    for nn in range(2):
                        cs = slice(512 * nn, 512 * nn + 512)
                        nc.vector.tensor_tensor(x[:, t, cs], x[:, t, cs], DD[:, 2 * t + nn, :], ALU.add).then_inc(x_ready, 1)
                n.x += 1

            rdens = {}

            def prep_at(cols, k0, kts=4):
                for b in range(kts // 2):
                    n.t[b % 2] += 1
                    n.xh += 1
                    dve.wait_ge(xh_done, n.xh)
                    for j in range(2):
                        k = k0 + 2 * b + j
                        ins = nc.vector.scalar_tensor_tensor(
                            out=xl[:, k, :], in0=TB[:, b % 2, j * S:(j + 1) * S], scalar=cols(j),
                            in1=xh[:, k, :].bitcast(F32), op0=ALU.mult, op1=ALU.subtract)
                    ins.then_inc(t_used[b % 2], 1)

            def trig_angles():
                dve.wait_ge(mix_loaded, 48)
                chain(nc.vector.tensor_copy(posf, posi[:, :]))
                for t in range(TT):
                    ins = nc.vector.tensor_scalar(ang[:, ROT * t:ROT * t + ROT], invf, posf[:, t:t + 1], None, ALU.mult)
                chain(ins)
                magic, c1, c2, c3 = 1.5 * 2.0 ** 23, 6.28125, 2029 / 2.0 ** 20, 2 * math.pi - 6.28125 - 2029 / 2.0 ** 20
                for i, turn in ((0, 0.0), (1, 0.25)):
                    ins = nc.vector.tensor_scalar(turns[:, 16 * i:16 * i + 16], ang, 1 / (2 * math.pi), turn, ALU.mult, ALU.add)
                chain(ins)
                chain(nc.vector.tensor_scalar(turns, turns, magic, -magic, ALU.add, ALU.add))
                for i in range(2):
                    ins = nc.vector.scalar_tensor_tensor(out=red[:, 16 * i:16 * i + 16], in0=turns[:, 16 * i:16 * i + 16], scalar=-c1,
                                                         in1=ang, op0=ALU.mult, op1=ALU.add)
                chain(ins)
                for c_ in (c2, c3):
                    chain(nc.vector.scalar_tensor_tensor(out=red, in0=turns, scalar=-c_, in1=red, op0=ALU.mult, op1=ALU.add))
                chain(nc.vector.tensor_scalar(red[:, 16:32], red[:, 16:32], math.pi / 2, None, ALU.add))
                nc.vector.tensor_scalar(red, red, 3.1415925, -3.1415925, ALU.min, ALU.max).then_inc(red_ready, 1)

            def rope():
                dve.wait_ge(trig_ready, 1)
                xb = P3(C_BQ, 20 * 64).rearrange("p t (h d) -> p t h d", d=64)
                t1, t2 = xb[:, :, :, 0:ROT], xb[:, :, :, ROT:2 * ROT]
                sin, cos = (trig[:, 16 * i:16 * i + 16].rearrange("p (t r) -> p t r", t=TT).unsqueeze(2).broadcast_to([P, TT, 20, ROT])
                            for i in range(2))
                a_, b_, c_ = (g1_[:, 320 * i:320 * i + 320].rearrange("p (t h r) -> p t h r", t=TT, r=ROT) for i in range(3))
                d_ = psc[:, 0, 0:320].rearrange("p (t h r) -> p t h r", t=TT, r=ROT)
                nc.vector.tensor_tensor(a_, t1, cos, ALU.mult)
                nc.vector.tensor_tensor(b_, t2, sin, ALU.mult)
                nc.vector.tensor_tensor(c_, t2, cos, ALU.mult)
                chain(nc.vector.tensor_tensor(d_, t1, sin, ALU.mult))
                for h0, h1 in ((0, 10), (12, 14), (16, 18)):
                    nc.vector.tensor_tensor(t1[:, :, h0:h1], a_[:, :, h0:h1], b_[:, :, h0:h1], ALU.subtract)
                    ins = nc.vector.tensor_tensor(t2[:, :, h0:h1], c_[:, :, h0:h1], d_[:, :, h0:h1], ALU.add)
                ins.then_inc(rope_ready, 1)
                dve.wait_ge(rope_ready, 1)
                for i, c0 in enumerate((C_KC, C_VC, C_KS, C_KW)):
                    for u in range(2):
                        ins = nc.vector.tensor_copy(kd[:, i, :, :, u, :], P3(c0, 128).rearrange("p t (g d) -> p t g d", g=2))
                ins.then_inc(kd_copied, 1)

            dve_setup()
            prep_x("pre0", "ffn0")
            ffn("ffn0", "pre0")
            post(0, "conv_in")
            prep_x("pre1", "conv_in")
            evacuate("pre1", "conv_in", 6, lambda g, t: P3(512 * g, 512, 0, 3072)[:, t, :], after=dve_cu)
            dve_conv()
            split_to(seg["conv_out"] + 4)
            post(1, "ffn1")
            prep_x("pre2", "ffn1")
            ffn("ffn1", "pre2")
            post(2, "kv")
            prep_x("pre3", "kv")
            evacuate("pre3", "kv", 4, kv_dst)
            dve_copy_transposed(kT)
            prep_x("pre4", "ffn2")
            ffn("ffn2", "pre4")
            post(3, "q")
            prep_x("pre5", "q")
            evacuate("pre5", "q", 2, kv_dst, scale=r8)
            dve_copy_transposed(qT)
            dve_attention()
            split_to(seg["o"] + 4)
            post(4, "ffn3")
            prep_x("pre6", "ffn3")
            ffn("ffn3", "pre6")
            post(5, "w_in")
            prep_x("pre7", "w_in")
            dve_mixers()
            prep_x("pre8", "ff")
            ffn("ff", "pre8")
            dve_final()

        @block.gpsimd
        def _(pool):
            count = [0]

            def chain(ins):
                count[0] += 1
                ins.then_inc(pool_chain, 1)
                pool.wait_ge(pool_chain, count[0])

            def norm(cols, s_, m_, r_, width, ready):
                chain(nc.gpsimd.tensor_scalar(m_, s_, 1.0 / width, EPS, ALU.mult, ALU.add))
                nc.gpsimd.tensor_tensor(r_, m_, nhalf[:, 0:cols], ALU.pow).then_inc(ready, 1)

            def norms(first, last):
                for name in NORMS[NORMS.index(first):NORMS.index(last) + 1]:
                    for t in range(TT):
                        c = ncol[name] + t
                        pool.wait_ge(ssq_ready, c + 1)
                        norm(1, ssq[:, c:c + 1], msq[:, c:c + 1], rs[:, c:c + 1], D, rs_ready)

            chain(nc.gpsimd.memset(ident[:, :], 0.0))
            nc.gpsimd.affine_select(out=ident[:, :], in_=ident[:, :], compare_op=ALU.not_equal, fill=1.0, base=0,
                                    pattern=[[-1, P]], channel_multiplier=1).then_inc(const_ready, 1)
            nc.gpsimd.memset(nhalf[:, :], -0.5)
            chain(nc.gpsimd.memset(mask3[:, :], 0.0))
            for lo_ in (0, 2 * P):
                ins = nc.gpsimd.affine_select(out=mask3[:, lo_:lo_ + P], in_=mask3[:, lo_:lo_ + P], compare_op=ALU.is_ge,
                                              fill=NEG, base=0, pattern=[[-1, P]], channel_multiplier=1)
            chain(ins)
            chain(nc.gpsimd.memset(cst[:, :], 1.0))
            nc.gpsimd.memset(coef[:, 0:S:CH], 0.0)
            chain(nc.gpsimd.affine_select(out=m64, in_=m64, compare_op=ALU.is_ge, fill=0.0, base=0,
                                          pattern=[[1, P]], channel_multiplier=-1))
            nc.gpsimd.memset(m64[0:CH, CH:P], 0.0)
            chain(nc.gpsimd.memset(cmask, 1.0))
            chain(nc.gpsimd.affine_select(out=cmask, in_=cmask, compare_op=ALU.is_ge, fill=0.0, base=-31,
                                          pattern=[[P, TT], [-16, NCMP]], channel_multiplier=1))
            nc.gpsimd.tensor_scalar(cneg, cmask, -1.0, -NEG, ALU.add, ALU.mult)
            chain(nc.gpsimd.memset(bdiag, 1.0))
            chain(nc.gpsimd.affine_select(out=bdiag, in_=bdiag, compare_op=ALU.is_ge, fill=0.0, base=0,
                                          pattern=[[-NCMP, 8]], channel_multiplier=1))
            chain(nc.gpsimd.affine_select(out=bdiag, in_=bdiag, compare_op=ALU.is_ge, fill=0.0, base=NCMP - 1,
                                          pattern=[[NCMP, 8]], channel_multiplier=-1))
            freqs = np.float32(500000.0) ** (-np.arange(0, 2 * ROT, 2, dtype=np.float32) / np.float32(2 * ROT))
            for i in range(ROT):
                ins = nc.gpsimd.memset(invf[:, i:i + 1], float(freqs[i]))
            ins.then_inc(const2, 1)
            norms("pre0", "pre5")
            pool.wait_ge(rs_ready, ncol["pre5"] + 2)
            nc.gpsimd.tensor_scalar(r8[:, :], rs[:, ncol["pre5"]:ncol["pre5"] + 2], 0.125, None, ALU.mult).then_inc(r8_ready, 1)
            for i in range(2):
                pool.wait_ge(oss_ready, i + 1)
                cols = slice(8 * i, 8 * i + 8)
                norm(8, oss[:, cols], omsq[:, cols], ro[:, cols], P, ro_ready)
            norms("post4", "pre7")
            pool.wait_ge(hss_ready, 1)
            norm(8, hss, hms, hr, P, hr_ready)
            norms("pre8", "final")


_NAMES = ["x", "g_norm", "w_ffn_gate", "w_ffn_up", "w_ffn_down", "w_conv_in", "w_conv", "w_conv_out", "g_kv", "w_kv",
          "w_q", "lambda_q1", "lambda_k1", "lambda_q2", "lambda_k2", "g_subln", "w_o", "positions_2", "norm1_g_2",
          "w_in_2", "lb_param_2", "hgrn_norm_g_2", "cmp_pe_k_2", "cmp_pe_v_2", "cmp_w1_k_2", "cmp_w2_k_2",
          "cmp_w1_v_2", "cmp_w2_v_2", "w_br_a_2", "w_br_b_2", "w_out_2", "norm2_g_2", "w_ff1_2", "w_ff2_2",
          "final_g_2"]


def kernel(**inputs):
    import numpy as _np
    import concourse.bacc as _bacc
    from concourse import mybir as _mybir
    from concourse.bass_utils import run_bass_kernel_spmd as _run

    nc = _bacc.Bacc("TRN2", target_bir_lowering=False, num_devices=1, dynamic_dma_scratch_size=1024)
    arrays, args = {}, {}
    for name in _NAMES:
        v = _np.ascontiguousarray(inputs[name])
        arrays[f"in_{name}"] = v
        args[name] = nc.dram_tensor(f"in_{name}", v.shape, _mybir.dt.from_np(v.dtype), kind="ExternalInput").ap()
    out = nc.dram_tensor("out_0", (1, S, D), F32, kind="ExternalOutput").ap()
    two_blocks(nc, args, out)
    return _run(nc, [arrays], core_ids=[0]).results[0]["out_0"]
```
